# Optimizing a Trainium2 kernel written in Bass

```python
import math
import jax
import jax.numpy as jnp
from jax import lax
import numpy as np

D_MODEL = 1024
BATCH = 1
SEQ = 256
DEPTH = 2
DEC_BATCH = 1
DEC_SEQ = 512
PAST_LEN = 128

F32 = jnp.float32
NORM_EPS = 1e-6
HEAD_DIM = 64
ROT_DIM = HEAD_DIM // 4
ROPE_THETA = 500000.0

A_PATTERNS = ((128, 1), (512, 4), (2048, 16))
A_GROUPS = len(A_PATTERNS)
A_HEADS = 6
A_WIDTH = A_HEADS * HEAD_DIM
A_QKV = A_GROUPS * A_WIDTH

B_HEADS = 4
B_HEAD_DIM = 128
B_WIDTH = B_HEADS * B_HEAD_DIM
B_CONV = 3
B_CHUNK = 64

C_HEADS = 4
C_QK_DIM = HEAD_DIM
C_V_DIM = 2 * C_QK_DIM
C_QK_WIDTH = C_HEADS * 2 * C_QK_DIM
C_WIDTH = C_HEADS * C_V_DIM
C_QBLK = 128

N_BRANCH = 3
BRANCH_WIDTH = A_WIDTH + B_WIDTH + C_WIDTH
D_FF = -(-8 * D_MODEL // (3 * 256)) * 256

IN_SPLITS = (A_QKV, A_QKV, A_QKV, B_WIDTH, B_WIDTH, B_WIDTH, 4 * B_HEADS,
             C_QK_WIDTH, C_QK_WIDTH, C_WIDTH, N_BRANCH * D_MODEL)
IN_COLS = sum(IN_SPLITS)
IN_OFFSETS = tuple(int(v) for v in np.cumsum(IN_SPLITS)[:-1])

kernel_name = "hybrid_dilated_mlstm_diffattn_encoder"

def rms_norm(x, g):
    xf = x.astype(F32)
    y = xf * lax.rsqrt(jnp.mean(xf * xf, axis=-1, keepdims=True) + NORM_EPS)
    return (y * g.astype(F32)).astype(x.dtype)

def rotary_tables(seq, dtype):
    inv = ROPE_THETA ** (-jnp.arange(0, ROT_DIM, 2, dtype=F32) / ROT_DIM)
    ang = jnp.arange(seq, dtype=F32)[:, None] * inv[None, :]
    return jnp.cos(ang).astype(dtype), jnp.sin(ang).astype(dtype)

def partial_rotary(x, cos, sin):
    extra = x.ndim - 3
    c = cos.reshape(cos.shape[0], *([1] * extra), cos.shape[1])
    s = sin.reshape(sin.shape[0], *([1] * extra), sin.shape[1])
    half = ROT_DIM // 2
    x1, x2, xp = x[..., :half], x[..., half:ROT_DIM], x[..., ROT_DIM:]
    return jnp.concatenate([x1 * c - x2 * s, x2 * c + x1 * s, xp], axis=-1)

def dilated_window_attention(q, k, v, dilation, half):
    Bn, S, H, Dh = q.shape
    L = S // dilation
    nb = -(-L // half)
    Lp = nb * half

    def to_strided(t):
        return t.reshape(Bn, L, dilation, H, Dh).transpose(0, 2, 3, 1, 4)

    qs, ks, vs = to_strided(q), to_strided(k), to_strided(v)
    qb = jnp.pad(qs, ((0, 0), (0, 0), (0, 0), (0, Lp - L), (0, 0))).reshape(Bn, dilation, H, nb, half, Dh)
    pad_kv = ((0, 0), (0, 0), (0, 0), (half, Lp - L + half), (0, 0))
    kp, vp = jnp.pad(ks, pad_kv), jnp.pad(vs, pad_kv)

    def windows(t):
        return jnp.concatenate(
            [t[:, :, :, j * half:j * half + Lp].reshape(Bn, dilation, H, nb, half, Dh) for j in range(3)], axis=4)

    kw, vw = windows(kp), windows(vp)
    s = jnp.einsum('brhnqd,brhnkd->brhnqk', qb, kw).astype(F32) * (1.0 / math.sqrt(Dh))
    qpos = jnp.arange(nb)[:, None, None] * half + jnp.arange(half)[None, :, None]
    kpos = jnp.arange(nb)[:, None, None] * half + jnp.arange(3 * half)[None, None, :] - half
    mask = (kpos >= 0) & (kpos < L) & (jnp.abs(qpos - kpos) <= half)
    s = jnp.where(mask, s, -1e30)
    mx = jnp.max(s, axis=-1, keepdims=True)
    p = jnp.exp(s - mx)
    den = jnp.sum(p, axis=-1, keepdims=True)
    o = jnp.einsum('brhnqk,brhnkd->brhnqd', (p / den).astype(v.dtype), vw)
    lse = (mx + jnp.log(den))[..., 0]
    o = o.reshape(Bn, dilation, H, Lp, Dh)[:, :, :, :L].transpose(0, 3, 1, 2, 4).reshape(Bn, S, H, Dh)
    lse = lse.reshape(Bn, dilation, H, Lp)[:, :, :, :L].transpose(0, 3, 1, 2).reshape(Bn, S, H)
    return o, lse

def mlstm_chunkwise(q, k, v, log_i, log_f):
    Bn, H, S, Dh = q.shape
    L = B_CHUNK
    nc = S // L

    def chunks(t):
        return jnp.moveaxis(t.astype(F32).reshape(Bn, H, nc, L, *t.shape[3:]), 2, 0)

    xs = (chunks(q), chunks(k), chunks(v), chunks(log_i), chunks(log_f))
    tri = jnp.tril(jnp.ones((L, L), dtype=bool))

    def step(carry, inp):
        C, n, m = carry
        qt, kt, vt, li, lf = inp
        b = jnp.cumsum(lf, axis=-1)
        b_last = b[..., -1]
        logD = jnp.where(tri, b[..., :, None] - b[..., None, :] + li[..., None, :], -jnp.inf)
        inter = b + m[..., None]
        m_t = jnp.maximum(inter, jnp.max(logD, axis=-1))
        sc = jnp.einsum('bhtd,bhsd->bhts', qt, kt) * jnp.exp(logD - m_t[..., None])
        w_inter = jnp.exp(inter - m_t)
        num = w_inter[..., None] * jnp.einsum('bhtd,bhde->bhte', qt, C) + jnp.einsum('bhts,bhse->bhte', sc, vt)
        den = w_inter * jnp.einsum('bhtd,bhd->bht', qt, n) + jnp.sum(sc, axis=-1)
        h = num / jnp.maximum(jnp.abs(den), jnp.exp(-m_t))[..., None]
        g = b_last[..., None] - b + li
        m_new = jnp.maximum(b_last + m, jnp.max(g, axis=-1))
        decay = jnp.exp(b_last + m - m_new)
        wk = jnp.exp(g - m_new[..., None])[..., None] * kt
        C_new = decay[..., None, None] * C + jnp.einsum('bhsd,bhse->bhde', wk, vt)
        n_new = decay[..., None] * n + jnp.sum(wk, axis=2)
        return (C_new, n_new, m_new), h

    init = (jnp.zeros((Bn, H, Dh, Dh), F32), jnp.zeros((Bn, H, Dh), F32), jnp.zeros((Bn, H), F32))
    _, hs = lax.scan(step, init, xs)
    return jnp.moveaxis(hs, 0, 2).reshape(Bn, H, S, Dh)

def diff_attention(q, k, v, lam):
    Bn, S, H, _, dk = q.shape
    dv = v.shape[-1]
    nq = S // C_QBLK
    qb = jnp.moveaxis(q.reshape(Bn, nq, C_QBLK, H, 2, dk), 1, 0)
    scale = 1.0 / math.sqrt(dk)

    def block(qblk):
        s = jnp.einsum('bqhmd,bkhmd->bhmqk', qblk, k).astype(F32) * scale
        p = jax.nn.softmax(s, axis=-1)
        a = p[:, :, 0] - lam * p[:, :, 1]
        return jnp.einsum('bhqk,bkhe->bqhe', a.astype(v.dtype), v)

    o = lax.map(block, qb)
    return jnp.moveaxis(o, 0, 1).reshape(Bn, S, H, dv)

def encoder_layer(x, layer_idx, norm1_g, w_in, a_qn_g, a_kn_g, b_conv_w, b_conv_b, b_wq, b_wk, b_gate_bias,
                  b_hn_g, c_qn_g, c_kn_g, c_lambda, c_hn_g, w_branch, w_out, norm2_g, w_ffn_in, w_ffn_out):
    Bn, S, _ = x.shape
    dt = x.dtype
    cos, sin = rotary_tables(S, dt)
    xn = rms_norm(x, norm1_g)
    proj = xn @ w_in
    (a_q, a_k, a_v, b_c, b_v, b_o, b_g, c_q, c_k, c_v, gate_pre) = jnp.split(proj, IN_OFFSETS, axis=-1)

    shp = (Bn, S, A_GROUPS, A_HEADS, HEAD_DIM)
    qa = partial_rotary(rms_norm(a_q.reshape(shp), a_qn_g), cos, sin)
    ka = partial_rotary(rms_norm(a_k.reshape(shp), a_kn_g), cos, sin)
    va = a_v.reshape(shp)
    outs, lses = [], []
    for g, (window, dil) in enumerate(A_PATTERNS):
        o_g, l_g = dilated_window_attention(qa[:, :, g], ka[:, :, g], va[:, :, g], dil, window // (2 * dil))
        outs.append(o_g)
        lses.append(l_g)
    alpha = jax.nn.softmax(jnp.stack(lses, axis=0), axis=0)
    o_a = jnp.sum(alpha[..., None] * jnp.stack(outs, axis=0).astype(F32), axis=0).astype(dt)
    o_a = o_a.reshape(Bn, S, A_WIDTH)

    pad = B_CONV // 2
    cp = jnp.pad(b_c, ((0, 0), (pad, pad), (0, 0)))
    conv = b_conv_b
    for j in range(B_CONV):
        conv = conv + cp[:, j:j + S] * b_conv_w[j]
    u = jax.nn.silu(conv).reshape(Bn, S, B_HEADS, B_HEAD_DIM)
    qb = jnp.einsum('bshd,hde->bhse', u, b_wq)
    kb = jnp.einsum('bshd,hde->bhse', u, b_wk) * (1.0 / math.sqrt(B_HEAD_DIM))
    vb = b_v.reshape(Bn, S, B_HEADS, B_HEAD_DIM).transpose(0, 2, 1, 3)
    gts = (b_g.astype(F32).reshape(Bn, S, 4, B_HEADS) + b_gate_bias.astype(F32)).transpose(2, 0, 3, 1)
    h_fwd = mlstm_chunkwise(qb, kb, vb, gts[0], jax.nn.log_sigmoid(gts[1]))
    flip = lambda t: jnp.flip(t, axis=2)
    h_bwd = flip(mlstm_chunkwise(flip(qb), flip(kb), flip(vb), flip(gts[2]), jax.nn.log_sigmoid(flip(gts[3]))))
    hb = (h_fwd + h_bwd).transpose(0, 2, 1, 3)
    hb = rms_norm(hb, b_hn_g.reshape(B_HEADS, B_HEAD_DIM)).astype(dt)
    o_b = jax.nn.sigmoid(b_o) * hb.reshape(Bn, S, B_WIDTH)

    cshp = (Bn, S, C_HEADS, 2, C_QK_DIM)
    qc = partial_rotary(rms_norm(c_q.reshape(cshp), c_qn_g), cos, sin)
    kc = partial_rotary(rms_norm(c_k.reshape(cshp), c_kn_g), cos, sin)
    vc = c_v.reshape(Bn, S, C_HEADS, C_V_DIM)
    lam_init = 0.8 - 0.6 * math.exp(-0.3 * layer_idx)
    lf = c_lambda.astype(F32)
    lam = jnp.exp(jnp.sum(lf[0] * lf[1])) - jnp.exp(jnp.sum(lf[2] * lf[3])) + lam_init
    o_c = diff_attention(qc, kc, vc, lam)
    o_c = (rms_norm(o_c, c_hn_g) * (1.0 - lam_init)).reshape(Bn, S, C_WIDTH)

    gates = jax.nn.sigmoid(gate_pre).reshape(Bn, S, N_BRANCH, D_MODEL)
    y_a = o_a @ w_branch[:A_WIDTH]
    y_b = o_b @ w_branch[A_WIDTH:A_WIDTH + B_WIDTH]
    y_c = o_c @ w_branch[A_WIDTH + B_WIDTH:]
    mixed = gates[:, :, 0] * y_a + gates[:, :, 1] * y_b + gates[:, :, 2] * y_c
    x = x + mixed @ w_out

    hg, hu = jnp.split(rms_norm(x, norm2_g) @ w_ffn_in, 2, axis=-1)
    return x + (jax.nn.silu(hg) * hu) @ w_ffn_out

def run_trunk(x, weights):
    for layer in range(DEPTH):
        x = encoder_layer(x, layer, *[w[layer] for w in weights])
    return x

def setup_inputs(seed: int = 0) -> dict:
    key = jax.random.key(seed)
    ks = jax.random.split(key, 24)

    def nrm(k, shape, scale):
        return jax.random.normal(k, shape, F32) * scale

    def gain(k, shape):
        return 1.0 + 0.05 * jax.random.normal(k, shape, F32)

    forget_mask = jnp.array([0.0, 1.0, 0.0, 1.0], F32)[None, :, None]
    forget_init = jnp.linspace(3.0, 6.0, B_HEADS, dtype=F32)[None, None, :]
    return {
        "x_prompt": nrm(ks[0], (BATCH, SEQ, D_MODEL), 1.0),
        "x_sample": nrm(ks[1], (DEC_BATCH, DEC_SEQ, D_MODEL), 1.0),
        "norm1_g": gain(ks[2], (DEPTH, D_MODEL)),
        "w_in": nrm(ks[3], (DEPTH, D_MODEL, IN_COLS), D_MODEL ** -0.5),
        "a_qn_g": gain(ks[4], (DEPTH, HEAD_DIM)),
        "a_kn_g": gain(ks[5], (DEPTH, HEAD_DIM)),
        "b_conv_w": nrm(ks[6], (DEPTH, B_CONV, B_WIDTH), B_CONV ** -0.5),
        "b_conv_b": nrm(ks[7], (DEPTH, B_WIDTH), 0.02),
        "b_wq": nrm(ks[8], (DEPTH, B_HEADS, B_HEAD_DIM, B_HEAD_DIM), B_HEAD_DIM ** -0.5),
        "b_wk": nrm(ks[9], (DEPTH, B_HEADS, B_HEAD_DIM, B_HEAD_DIM), B_HEAD_DIM ** -0.5),
        "b_gate_bias": nrm(ks[10], (DEPTH, 4, B_HEADS), 0.1) + forget_mask * forget_init,
        "b_hn_g": gain(ks[11], (DEPTH, B_WIDTH)),
        "c_qn_g": gain(ks[12], (DEPTH, C_QK_DIM)),
        "c_kn_g": gain(ks[13], (DEPTH, C_QK_DIM)),
        "c_lambda": nrm(ks[14], (DEPTH, 4, C_QK_DIM), 0.1),
        "c_hn_g": gain(ks[15], (DEPTH, C_V_DIM)),
        "w_branch": nrm(ks[16], (DEPTH, BRANCH_WIDTH, D_MODEL), B_WIDTH ** -0.5),
        "w_out": nrm(ks[17], (DEPTH, D_MODEL, D_MODEL), D_MODEL ** -0.5),
        "norm2_g": gain(ks[18], (DEPTH, D_MODEL)),
        "w_ffn_in": nrm(ks[19], (DEPTH, D_MODEL, 2 * D_FF), D_MODEL ** -0.5),
        "w_ffn_out": nrm(ks[20], (DEPTH, D_FF, D_MODEL), D_FF ** -0.5),
    }

def reference(x_prompt, x_sample, norm1_g, w_in, a_qn_g, a_kn_g, b_conv_w, b_conv_b, b_wq, b_wk, b_gate_bias,
              b_hn_g, c_qn_g, c_kn_g, c_lambda, c_hn_g, w_branch, w_out, norm2_g, w_ffn_in, w_ffn_out):
    weights = (norm1_g, w_in, a_qn_g, a_kn_g, b_conv_w, b_conv_b, b_wq, b_wk, b_gate_bias, b_hn_g,
               c_qn_g, c_kn_g, c_lambda, c_hn_g, w_branch, w_out, norm2_g, w_ffn_in, w_ffn_out)
    y_prompt = run_trunk(x_prompt, weights)
    y_sample = run_trunk(x_sample, weights)
    return (y_prompt, y_sample)


_drawn_inputs = setup_inputs


def setup_inputs(seed=0):
    import zlib

    import numpy as np

    out = dict(_drawn_inputs(seed))
    spreads = {}
    factors = {'a_qn_g': 8.0, 'a_kn_g': 8.0}
    for name, (base, spread) in spreads.items():
        noise = np.random.default_rng([zlib.crc32(name.encode()), seed]).standard_normal(out[name].shape)
        drawn = base * np.exp(spread * noise) if base else spread * noise
        out[name] = jnp.asarray(drawn.astype(out[name].dtype))
    for name, factor in factors.items():
        out[name] = (out[name] * factor).astype(out[name].dtype)
    return out
```

```python
from contextlib import ExitStack

import concourse.bass as bass
from concourse import mybir
import numpy as np

F32 = mybir.dt.float32
F32R = mybir.dt.float32r
ALU = mybir.AluOpType
ACT = mybir.ActivationFunctionType
AX_X = mybir.AxisListType.X

P = 128
D = 1024
KD = D // P
DEPTH = 2
SEQS = ((0, 2), (2, 4))
NT = 6
TOK = NT * P
HALF_TOK = TOK // 2
EPS = 1e-6

HD = 64
ROT = 8
A_H = 6
A_G = 3
A_W = A_H * HD
A_DIL = (1, 4, 16)
B_H = 4
B_W = B_H * P
C_H = 4
C_W = C_H * P
D_FF = 2816
FF_TILES = D_FF // P
GROUPS = FF_TILES // 2
IN_COLS = 3 * A_G * A_W + 3 * B_W + 16 + 3 * C_W + 3 * D
COL_B = 3 * A_G * A_W
COL_BG = COL_B + 3 * B_W
COL_C = COL_BG + 16
COL_GATE = COL_C + 3 * C_W
MIX_ROWS = ((0, 3), (3, 4), (7, 4))

RAW = 3
SUB = 1024
OUT_PART = A_W + 2 * A_H


def chunk_list():
    chunks = []
    for g in range(A_G):
        for part in range(3):
            col = part * A_G * A_W + g * A_W
            chunks.append(("a", [("in", 2 * j, 2, col, A_W) for j in range(4)]))
    chunks.append(("bc", [("in", 0, 8, COL_B + h * P, P) for h in range(B_H)]))
    chunks.append(("bg", [("in", 0, 8, COL_BG, 16)]))
    for i in (1, 2):
        chunks.append(("bvo", [("in", 2 * j, 2, COL_B + i * B_W, B_W) for j in range(4)]))
    for i in range(3):
        chunks.append(("c", [("in", 2 * j, 2, COL_C + i * C_W, C_W) for j in range(4)]))
    for i in range(6):
        chunks.append(("gate", [("in", 0, 8, COL_GATE + (4 * i + j) * P, P) for j in range(4)]))
    for b, parts in ((0, ((0, 1), (2, 3))), (1, (range(4),)), (2, (range(4),))):
        for part in parts:
            chunks.append(("branch", [("branch", *MIX_ROWS[b], 2 * j * P, 2 * P) for j in part]))
    for h in range(2):
        chunks.append(("out", [("wout", 2 * j, 2, h * 512, 512) for j in range(4)]))
    return chunks


CHUNKS = chunk_list()
FIRST_SUB = [sum(len(s) for _, s in CHUNKS[:c]) for c in range(len(CHUNKS) + 1)]
C_BC, C_BG, C_BVO, C_C, C_GATE, C_BRANCH, C_OUT = 9, 10, 11, 13, 16, 22, 26
FFN_SUB0 = FIRST_SUB[-1]
WOUT = [(0, 0), (1, 0), (0, 1), (1, 1), (2, 0), (2, 1), (3, 0), (3, 1), (4, 0), (5, 0), (4, 1), (5, 1)]


def chunk_of(s):
    kind = s[0]
    if kind == "piece":
        return s[1], None
    if kind == "bc":
        return C_BC, s[1]
    if kind == "bg":
        return C_BG, 0
    if kind == "gate":
        return C_GATE + (8 * s[1] + s[2]) // 4, s[2] % 4
    if kind == "branch":
        b, j = s[1], s[2] // 2
        return (C_BRANCH + j // 2, j % 2) if b == 0 else (C_BRANCH + 1 + b, j)
    if kind == "wout":
        return C_OUT + s[2], None
    return None, None


GAP_A, GAP_B, GAP_C, ROUND = (1, 2, 4, 2.5), (4, 6, 4), (4, 5), 0.45


def prep_list():
    order, preps, units = [], [], []
    for g in range(A_G):
        for s, (t0, n) in enumerate(SEQS):
            base = len(preps)
            for t in range(n + (g == 0)):
                preps.append((g, s, t if t < n else None, t))
                u = t - 1 if g == 0 else t
                if u >= 0:
                    units.append((g, s, u, [base + u, base + u + 1] if g == 0 else [base + u]))
    loaded = folded = 0
    for u in range(len(units) + 1):
        while loaded < len(preps) and (loaded < 3 or 1 + max(
                i for i, x in enumerate(units) if loaded - 3 in x[3]) <= u):
            order.append((("a_load", loaded), 0))
            loaded += 1
        if u == len(units):
            break
        early = folded > units[u][3][-1]
        while folded <= units[u][3][-1]:
            order.append((("a_fold", folded), 8 if preps[folded][0] == 0 and preps[folded][3] == 0 else GAP_A[0]))
            folded += 1
        order.append((("a_score", u), 0 if early else GAP_A[1]))
        if len(units[u][3]) == 1 and u + 1 < len(units):
            order += [(("a_fold", folded), GAP_A[2]), (("a_turn", u), 0)]
            folded += 1
        else:
            order.append((("a_turn", u), GAP_A[2]))
        order.append((("a_out", u), GAP_A[3]))
    return preps, units, order


PREPS, UNITS, A_ORDER = prep_list()
LAST_USE = [1 + max(u for u, x in enumerate(UNITS) if p in x[3]) for p in range(len(PREPS))]


def token_rows(g, s, t, halo):
    t0, n = SEQS[s]
    base = t0 * P
    if halo:
        if t == 0:
            return [(64, 64, base, 1)]
        if t == n:
            return [(0, 64, base + P * n - 64, 1)]
        return [(0, P, base + P * t - 64, 1)]
    dil = A_DIL[g]
    length = n * P // dil if dil > 1 else P
    if dil == 1:
        return [(0, P, base + P * t, 1)]
    per = P // length
    return [(i * length, length, base + t * per + i, dil) for i in range(per)]


def tables():
    inv = (np.float32(500000.0) ** (-np.arange(0, 16, 2, dtype=np.float32) / np.float32(16))).astype(np.float32)
    pos = (P * np.arange(4)[None, :] + np.arange(P)[:, None]).astype(np.float32)
    ang = (pos[:, :, None] * inv[None, None, :]).astype(np.float32)
    rope = np.concatenate([np.cos(ang), np.sin(ang)], axis=2).astype(np.float32)
    r, c = np.arange(P)[:, None], np.arange(P)[None, :]
    up, low = c >= r, c <= r
    keep = [up & (c >= 64), up, low, low & (c < 64), abs(r - c) <= 64, r // 64 == c // 64,
            r // 32 == c // 32, r // 16 == c // 16]
    masks = np.stack([np.where(k, 0.0, -1e30) for k in keep], axis=1).astype(np.float32)
    lam = np.array([[0.8 - 0.6 * np.exp(-0.3 * i), 0.2 + 0.6 * np.exp(-0.3 * i)] for i in range(DEPTH)], np.float32)
    return {"t_rope": rope, "t_masks": masks, "t_ident": np.eye(P, dtype=np.float32),
            "t_lam": np.repeat(lam[:, None, :], P, axis=1).copy()}


def mask_of(g, s, t):
    if g == 0:
        return slice(0, 3, 2) if t == 0 else slice(1, 4, 2) if t == SEQS[s][1] - 1 else slice(1, 3)
    m = {(1, 1): 4, (1, 0): 5, (2, 1): 6, (2, 0): 7}[g, s]
    return slice(m, m + 1)


B_UNITS = [(s, h) for s in range(2) for h in range(B_H)]


def b_order():
    order = [(("b_rows",), 0), (("b_gates",), 8), (("b_scan", 0), 6), (("b_scan", 1), 4), (("b_scan", 2), 4), (("b_scan", 3), 4),
             (("b_columns",), 6),
             (("b_conv", 0), 0)]
    for u in range(len(B_UNITS)):
        order += [(("b_qk", u), GAP_B[0] if u else 12), (("b_decay", u), 0)]
        if u + 1 < len(B_UNITS):
            order.append((("b_conv", u + 1), 0))
        order += [(("b_score", u), GAP_B[1]), (("b_out", u), GAP_B[2])]
    return order


C_UNITS = [(s, t, h) for s, (t0, n) in enumerate(SEQS) for t in range(n) for h in range(C_H)]


def c_order():
    order, u0, p0 = [(("c_lambda",), 0)], 0, 0
    for s, (t0, n) in enumerate(SEQS):
        for t in range(n):
            order += [(("c_fold", p0 + t), GAP_C[0] if t else 14 - 5 * s)]
        m = n * C_H
        for i in range(m + 2):
            if i < m:
                order.append((("c_score", u0 + i), GAP_C[1]))
            if 1 <= i <= m:
                order.append((("c_turn", u0 + i - 1), 0 if i < m else 5))
            if i >= 2:
                order.append((("c_out", u0 + i - 2), 0 if i < m else 3))
                if (i - 2) % C_H == C_H - 1:
                    order.append((("c_norm", p0 + (i - 2) // C_H), 0))
        u0 += m
        p0 += n
    return order


C_PREPS = [(s, t) for s, (t0, n) in enumerate(SEQS) for t in range(n)]


def side_order():
    order = list(A_ORDER) + [(("a_merge", 0), 5)]
    for t in range(NT):
        order += [(("a_merge", t + 1), 0)] if t + 1 < NT else []
        order.append((("turn", 0, t), 6))
    order += b_order() + [(("turn_load", 1, 0), 0), (("turn_load", 1, 1), 0)] + c_order()
    return order


def dense_cost(s):
    if s[0] == "piece":
        return 3.9 if s[1] < 9 else 5.2
    if s[0] == "turn":
        return 0.8
    if s[0] == "turn_load":
        return 0
    if s[0] == "branch":
        return 0.97 * MIX_ROWS[s[1]][1]
    return 7.7


def side_needs(s):
    kind = s[0]
    if kind == "a_load":
        return ("piece", 3 * PREPS[s[1]][0] + 3, 1) if PREPS[s[1]][0] < 2 else ("bc", 1)
    if kind == "b_rows":
        return ("piece", C_C, 0)
    if kind == "c_lambda":
        return ("gate", 0, 0)
    return None


def schedule():
    steps = [("rms", 0), ("first", 0), ("first", 1), ("rms", 1), ("first", 2), ("first", 3), ("norm", 0), ("rms", 2),
             ("first", 4), ("first", 5), ("norm", 1), ("rms", 3), ("first", 6), ("first", 7)]
    for t in range(4):
        steps += [("piece", 0, t), ("norm", t + 2)] + ([("rms", t + 4)] if t < 2 else []) + [("piece", 1, t)]
    steps += [("piece", 0, 4), ("piece", 0, 5), ("piece", 1, 4), ("piece", 1, 5)]
    dense = [("piece", 2, t) for t in range(NT)] + [("piece", c, t) for c in range(3, 9) for t in range(NT)]
    dense += [("bc", h) for h in range(B_H)] + [("bg",)]
    dense += [("piece", c, t) for c in range(C_BVO, C_GATE) for t in range(NT)]
    dense += [("gate", b, d) for b in range(3) for d in range(KD)]
    for d in range(KD):
        dense.append(("branch", 0, d))
        if d < NT:
            dense.append(("turn", 1, d))
        if d + 2 < NT:
            dense.append(("turn_load", 1, d + 2))
    dense += [("branch", b, d) for b in (1, 2) for d in range(KD)]
    side, gone, since = side_order(), set(), 0
    late = [("turn_load", 2, 0), ("turn_load", 2, 1)]
    for t in range(NT):
        late += [("turn", 2, t)] + ([("turn_load", 2, t + 2)] if t + 2 < NT else [])
    loaded_at = {}
    while dense or side or late:
        if late:
            kind, _, t = late[0]
            free = ("turn", 1, NT - 1) in gone and ("c_norm", t) in gone
            if kind == "turn":
                free = free and ("branch", 0, KD - 1) in gone and (
                    len(steps) >= loaded_at[t] + 4 or not side and not dense)
                free = free or (not side and dense[0] == ("branch", 2, 0))
            if free:
                if kind == "turn_load":
                    loaded_at[t] = len(steps)
                steps.append(late.pop(0))
                gone.add(steps[-1])
                continue
        ready = bool(side) and (side_needs(side[0][0]) is None or side_needs(side[0][0]) in gone)
        d = dense[0] if dense else None
        blocked = d is None or (d[0] == "branch" and ("turn", d[1], NT - 1) not in gone) or (
            d[0] == "turn" and ("b_out", len(B_UNITS) - 1) not in gone)
        if ready and (blocked or since + ROUND * dense_cost(d) * (side[0][1] > 0) >= side[0][1]):
            step, gap = side.pop(0)
            if gap:
                since = 0
        else:
            assert not blocked, side[0]
            step = dense.pop(0)
            since += dense_cost(step)
        steps.append(step)
        gone.add(step)
    done = 0
    for i, (t, h) in enumerate(WOUT):
        steps.append(("wout", t, h))
        if (t, h) == (5, 0):
            steps.append(("ffn_split",))
        if done < NT and i >= WOUT.index((done, 1)):
            steps.append(("rms", NT + done))
            if done:
                steps.append(("norm", NT + done - 1))
            done += 1
    steps += [("rms", NT + t) for t in range(done, NT)] + [("norm", 2 * NT - 1)]
    return steps


STEPS = schedule()


DENSE = [s for s in STEPS if s[0] in ("piece", "bc", "bg", "gate", "branch", "turn", "wout")]
INDEX = {s: n for n, s in enumerate(DENSE)}
DONE_AT = [1 + max(n for s, n in INDEX.items() if chunk_of(s)[0] == c) for c in range(len(CHUNKS))]
STAGED = [s for s in DENSE if s[0] in ("piece", "bc", "bg", "gate", "branch")]
STAGE = {s: m for m, s in enumerate(STAGED)}
STORES = len(STAGED) - KD
HEADS = {s: i for i, s in enumerate([s for s in STAGED if s[0] == "piece" and (
    s[1] % 3 < 2 if s[1] < 9 else s[1] in (C_C, C_C + 1))])}
PLAIN = {s: i for i, s in enumerate([s for s in STAGED if s not in HEADS and s[0] != "branch"])}


def split_plan():
    plan = {}
    for c in range(2, len(CHUNKS)):
        before = [s for s in DENSE[DONE_AT[c - 2]:] if chunk_of(s)[0] == c - 1]
        before = [s for s in before if INDEX[s] < min(n for x, n in INDEX.items() if chunk_of(x)[0] == c)]
        subs = list(range(FIRST_SUB[c], FIRST_SUB[c + 1]))
        for j, n in enumerate(subs):
            plan.setdefault(before[j * len(before) // len(subs)], []).append((c, n))
    return plan


SPLITS = split_plan()


class Tally:

    def __init__(self, eng, sem):
        self.eng, self.sem, self.n, self.base = eng, sem, 0, 0

    def __call__(self, ins):
        ins.then_inc(self.sem, 1)
        self.n += 1

    def wait(self):
        self.eng.wait_ge(self.sem, self.base + self.n)

    def link(self, ins):
        self(ins)
        self.wait()


def build(nc, io):
    ctx = ExitStack()
    with ctx:
        def sb(name, shape, dt=F32):
            return ctx.enter_context(nc.sbuf_tensor(name, shape, dt))

        def sem(name):
            s = ctx.enter_context(nc.semaphore(name))
            sems.append(s)
            return s

        sems = []

        def dram(name, shape):
            return nc.dram_tensor(name, shape, F32, kind="Internal").ap()

        qkv_a = dram("qkv_a", (TOK, 3, A_G, A_W))
        parts_a = dram("parts_a", (TOK, A_G, OUT_PART))
        conv_in = dram("conv_in", (B_W, TOK))
        b_vo = dram("b_vo", (TOK, 2, B_H, P))
        qkv_c = dram("qkv_c", (TOK, 3, C_W))
        o_tok = dram("o_tok", (2, TOK, B_W))
        gates_b = dram("gates_b", (16, TOK))
        gate_t = dram("gate_t", (3, D, TOK))
        mix_t = dram("mix_t", (D, TOK))
        x_save = dram("x_save", (TOK, D))

        xh, xl = sb("xh", [P, KD, TOK], F32R), sb("xl", [P, KD, TOK], F32R)
        wh, wl = sb("wh", [P, 2, 4, SUB], F32R), sb("wl", [P, 2, 4, SUB], F32R)
        oh, ol = sb("oh", [P, 4, TOK], F32R), sb("ol", [P, 4, TOK], F32R)
        wraw = sb("wraw", [P, RAW, SUB])
        ident = sb("ident", [P, P])
        masks = sb("masks", [P, 8, P])
        rope = sb("rope", [P, 4, 16])
        wide = sb("wide", [P, D])
        stage = sb("stage", [P, 2, TOK])
        eps = sb("eps", [P, 1])
        a_gain = sb("a_gain", [P, 2, HD])
        c_gain = sb("c_gain", [P, 2, HD])
        c_hgain = sb("c_hgain", [P, P])
        gate_bias = sb("gate_bias", [P, 4])
        conv_w = sb("conv_w", [P, 3, B_H])
        conv_b = sb("conv_b", [P, B_H])
        lam_c = sb("lam_c", [P, 2])
        lam = sb("lam", [P, 4])
        norm_s = sb("norm_s", [P, 2, 4])
        head_s = sb("head_s", [P, 2, 8])
        rot = sb("rot", [P, 2, 8, 2, ROT])
        unit_s = sb("unit_s", [P, 64])
        arena_floats = 10400
        arena = sb("arena", [P, arena_floats])
        ps = ctx.enter_context(nc.psum_tensor("ps", [P, 8, 512], F32))

        used = {}

        def area(phase, n):
            at = used.get(phase, 0)
            used[phase] = at + n
            assert at + n <= arena_floats, (phase, at + n)
            return arena[:, at:at + n]

        x = area("x", NT * D).rearrange("p (t d) -> p t d", t=NT)
        xn = area("x", 2 * D).rearrange("p (r d) -> p r d", r=2)
        x_sq = area("x", D)
        part_mix = arena[:, NT * D:NT * D + 2 * TOK].rearrange("p (r n) -> p r n", r=2)
        mix_raw = arena[:, NT * D + 2 * TOK:NT * D + 4 * TOK].rearrange("p (r n) -> p r n", r=2)
        f_e = arena[:, NT * D:NT * D + 2 * TOK].rearrange("p (r n) -> p r n", r=2)
        f_h = arena[:, NT * D + 2 * TOK:NT * D + 4 * TOK].rearrange("p (r n) -> p r n", r=2)
        a_in = area("a", 3 * 3 * A_W).rearrange("p (r i n) -> p r i n", r=3, i=3)
        a_qk = area("a", 3 * 2 * A_W).rearrange("p (r i n) -> p r i n", r=3, i=6)
        a_p = area("a", A_H * 2 * P)
        a_pt = area("a", A_H * 2 * P)
        a_o = area("a", 2 * OUT_PART).rearrange("p (r n) -> p r n", r=2)
        m_in = area("am", 2 * A_G * OUT_PART).rearrange("p (r g n) -> p r g n", r=2, g=A_G)
        m_w = area("am", 64)
        m_sc = area("am", A_G * A_W).rearrange("p (g h c) -> p g h c", g=A_G, h=A_H)
        m_o = area("am", 2 * A_W).rearrange("p (r n) -> p r n", r=2)
        nmx = area("b", 2 * TOK).rearrange("p (d n) -> p d n", d=2)
        used["bg"] = used["b"]
        b_w = area("b", 2 * B_W).rearrange("p (i h e) -> p i h e", i=2, h=B_H)
        b_hg = area("b", B_W)
        b_g = area("b", 48).rearrange("p (d t h) -> p d t h", d=2, t=NT)
        b_fl = area("b", 48).rearrange("p (d t h) -> p d t h", d=2, t=NT)
        b_c = area("b", 4 * P + 2)
        b_u = area("b", 4 * P)
        b_t = area("b", 4 * P)
        b_q = area("b", 4 * P)
        b_k = area("b", 4 * P)
        b_v = area("b", 4 * (P + 1)).rearrange("p (t e) -> p t e", t=4)
        b_og = area("b", 4 * P).rearrange("p (t e) -> p t e", t=4)
        b_d = area("b", 2 * 10 * P).rearrange("p (d n) -> p d n", d=2)
        b_o = area("b", 4 * P).rearrange("p (t e) -> p t e", t=4)
        g_li = area("bg", 2 * TOK).rearrange("p (d n) -> p d n", d=2)
        g_lf = area("bg", 2 * TOK).rearrange("p (d n) -> p d n", d=2)
        g_f = area("bg", 2 * TOK).rearrange("p (d n) -> p d n", d=2)
        g_zero = area("bg", 4 * P)
        c_kt = area("c", C_H * 4 * P).rearrange("p (h n) -> p h n", h=C_H)
        c_qt = area("c", C_H * 4 * P).rearrange("p (h n) -> p h n", h=C_H)
        c_v = area("c", 4 * C_W).rearrange("p (t n) -> p t n", t=4)
        c_in = area("c", 2 * C_W)
        c_tmp = area("c", C_W)
        c_e = area("c", 2 * 4 * P).rearrange("p (m n) -> p m n", m=2)
        c_at = area("c", 4 * P)
        c_o = area("c", C_W)
        turn_in = wide[:, :].rearrange("p (r n) -> p r n", r=2)

        side = ps[:, 4:8, :].rearrange("p b n -> p (b n)")

        const_in = sem("const_in")
        a_gain_in = sem("a_gain_in")
        gain1_in = sem("gain1_in")
        gain2_in = sem("gain2_in")
        w_in_s = [sem(f"w_loaded{r}") for r in range(RAW)]
        w_hi = sem("w_hi")
        w_lo = sem("w_lo")
        d_done = sem("d_done")
        act_staged = sem("act_staged")
        mixed = sem("mixed")
        stored = [sem(f"stored{i}") for i in range(2)]
        gate_in = [sem(f"gate_in{i}") for i in range(2)]
        part_in = [sem(f"part_in{i}") for i in range(2)]
        act_c, dve_c = sem("act_chain"), sem("dve_chain")
        n_rstd, n_xn, n_tr, n_hi, n_lo = (sem(x) for x in ("n_rstd", "n_xn", "n_tr", "n_hi", "n_lo"))
        x_saved, x_back = sem("x_saved"), sem("x_back")
        t_in = [sem(f"t_in{i}") for i in range(2)]
        t_hi = sem("t_hi")
        t_lo = sem("t_lo")
        a_loaded = [sem(f"a_loaded{i}") for i in range(3)]
        a_edge = sem("a_edge")
        h_sq, h_ss, h_rstd, h_scaled, h_ready = (sem("h_" + x) for x in ("sq", "ss", "rstd", "scaled", "ready"))
        a_tr, a_qkt, a_sc, a_mx, a_pr = (sem(x) for x in ("a_tr", "a_qkt", "a_sc", "a_mx", "a_pr"))
        a_ptr, a_pta, a_ptd, a_pv, a_ov = (sem(x) for x in ("a_ptr", "a_pta", "a_ptd", "a_pv", "a_ov"))
        a_stored = [sem(f"a_stored{i}") for i in range(2)]
        m_loaded = [sem(f"m_loaded{i}") for i in range(2)]
        m_dif, m_exp, m_out = (sem(x) for x in ("m_dif", "m_exp", "m_out"))
        bg_in, bg_abs, bg_ln, bg_scan, bg_col, bg_cols = (
            sem(x) for x in ("bg_in", "bg_abs", "bg_ln", "bg_scan", "bg_col", "bg_cols"))
        b_cin, b_win, b_vin = sem("b_cin"), sem("b_win"), sem("b_vin")
        b_conv, b_exp, b_u_s, b_qk, b_qke, b_bc, b_dg, b_dec, b_sc, b_wt, b_nd, b_h, b_sq, b_ssq, b_rs, b_fin = (
            sem("b_" + x) for x in ("conv", "exp", "u", "qk", "qke", "bc", "dg", "dec", "sc", "wt", "nd", "h", "sq",
                                    "ssq", "rs", "fin"))
        b_oge = sem("b_oge")
        b_store = sem("b_store")
        c_lin = sem("c_lin")
        c_vin = sem("c_vin")
        c_lamin = sem("c_lamin")
        c_lam = sem("c_lam")
        c_tr, c_qkt, c_sc, c_mx, c_ex, c_a, c_ptr, c_pt, c_pv, c_ov = (
            sem("c_" + x) for x in ("tr", "qkt", "sc", "mx", "ex", "a", "ptr", "pt",
                                    "pv", "ov"))
        co_sq, co_ss, co_rs, co_n = (sem("co_" + x) for x in ("sq", "ss", "rs", "n"))
        c_store = sem("c_store")
        r_hi, r_lo = sem("r_hi"), sem("r_lo")
        x_new = sem("x_new")
        f_in, f_ex, f_hf, f_hi, f_lo, f_out, f_add, f_ch = (
            sem("f_" + x) for x in ("in", "ex", "hf", "hi", "lo", "out", "add", "ch"))

        A_STORES, cnt = [], [0, 0]
        for u, (g, s, t, _) in enumerate(UNITS):
            cnt[u % 2] += len(token_rows(g, s, t, False))
            A_STORES.append(tuple(cnt))
        A_LOADS, A_EDGES, cnt, edges = [], [], [0, 0, 0], 0
        for p, (g, s, tq, tk) in enumerate(PREPS):
            kv = token_rows(g, s, tk, g == 0)
            cnt[p % 3] += len(kv) + (g == 0 and tq is not None)
            edges += g == 0 and kv[0][1] < P
            A_LOADS.append(cnt[p % 3])
            A_EDGES.append(edges)

        FREED = []
        for n, s in enumerate(DENSE):
            kind = s[0]
            if s in HEADS:
                FREED.append((h_scaled, HEADS[s] + 1))
            elif s in PLAIN:
                FREED.append((act_staged, PLAIN[s] + 1))
            elif kind == "branch":
                FREED.append((mixed, 8 * s[1] + s[2] + 1))
            elif kind == "turn":
                FREED.append((t_lo, NT * s[1] + s[2] + 1))
            else:
                FREED.append((x_new, WOUT.index(s[1:]) + 1))

        def decay(n, d, j):
            if d == 0:
                at = sum(n - i for i in range(j)) * P
                dm = b_d[:, 0, at:at + (n - j) * P]
                return dm, dm[:, 0:P]
            at = sum(i + 1 for i in range(j)) * P
            dm = b_d[:, 1, at:at + (j + 1) * P]
            return dm, dm[:, j * P:(j + 1) * P]

        def score_bank(nk, h):
            per = 4 // nk
            at = 512 * (nk * (h % 2) + h // 2 // per) + P * nk * (h // 2 % per)
            return side[:, at:at + nk * P]

        def turned(nk):
            return 0 if nk == 2 else 1024

        def unit_out(u):
            return 1536 if len(UNITS[u][3]) == 2 else 1024

        def ps_pair(n):
            return ps[:, 2 * (n % 2):2 * (n % 2) + 2, :]

        start = ctx.enter_context(nc.semaphore("start"))
        with nc.Block() as block:
            @block.sync
            def _(sp):
                sp.dma_start(ident[:, :], io["t_ident"]).then_inc(start, 16)
                sp.dma_start(masks[:, :, :], io["t_masks"]).then_inc(start, 16)
                sp.dma_start(rope[:, :, :], io["t_rope"]).then_inc(start, 16)
                xp = io["x_prompt"].rearrange("b (t p) d -> p (b t) d", p=P)
                xs = io["x_sample"].rearrange("b (t p) d -> p (b t) d", p=P)
                sp.dma_start(x[:, 0:2, :], xp).then_inc(start, 16)
                sp.dma_start(x[:, 2:NT, :], xs).then_inc(start, 16)
                sp.wait_ge(start, 80)

            @block.vector
            def _(dve):
                dve.memset(eps[:, :], EPS)

        with nc.Fori(0, DEPTH) as layer:
            with nc.Block() as block:
                w_of = {
                    "in": io["w_in"].rearrange("l (k p) n -> l p k n", p=P),
                    "branch": io["w_branch"].rearrange("l (k p) n -> l p k n", p=P),
                    "wout": io["w_out"].rearrange("l (k p) n -> l p k n", p=P),
                }
                w_gu = io["w_ffn_in"].rearrange("l (k p) (u f n) -> l u f p k n", p=P, u=2, n=P)
                w_dn = io["w_ffn_out"].rearrange("l (f p) n -> l f p n", p=P)

                def in_sub(a):
                    return FFN_SUB0 + 10 + 6 * (a - 2)

                def out_sub(a):
                    return FFN_SUB0 + 14 + 6 * (a - 1)

                def ffn(step_in, step_out, eng, tallies=()):
                    step_in(0, 0, FFN_SUB0, 0, "first")
                    step_in(0, 1, FFN_SUB0 + 4, 1, "second")
                    step_out(0, 0, FFN_SUB0 + 8, 0, "body")
                    turns = (GROUPS - 3) // 2
                    before = [t.n for t in tallies]
                    with eng.Fori(0, turns) as i:
                        for t in tallies:
                            t.base = i * t.per
                        step_in(i, 2, in_sub(2), 0, "body")
                        step_out(i, 1, out_sub(1), 1, "body")
                        step_in(i, 3, in_sub(3), 1, "body")
                        step_out(i, 2, out_sub(2), 0, "body")
                    for t, n in zip(tallies, before):
                        assert t.n - n == t.per, (t.n - n, t.per)
                        t.base, t.n = 0, n + t.per * turns
                    step_in(0, GROUPS - 1, in_sub(GROUPS - 1), 0, "body")
                    step_out(0, GROUPS - 2, out_sub(GROUPS - 2), 1, "before last")
                    step_out(0, GROUPS - 1, out_sub(GROUPS - 2) + 2, 0, "last")

                @block.sync
                def _(sp):
                    bc = lambda ap: ap.partition_broadcast(P)
                    sp.dma_start(wide[:, :], bc(io["norm1_g"][layer])).then_inc(gain1_in, 16)

                    sp.dma_start(a_gain[:, 0, :], bc(io["a_qn_g"][layer])).then_inc(a_gain_in, 16)
                    sp.dma_start(a_gain[:, 1, :], bc(io["a_kn_g"][layer])).then_inc(a_gain_in, 16)

                    def small_loads():
                        sp.dma_start(c_gain[:, 0, :], bc(io["c_qn_g"][layer])).then_inc(const_in, 16)
                        sp.dma_start(c_gain[:, 1, :], bc(io["c_kn_g"][layer])).then_inc(const_in, 16)
                        sp.dma_start(c_hgain[:, :], bc(io["c_hn_g"][layer])).then_inc(const_in, 16)
                        sp.dma_start(gate_bias[0:4, :], io["b_gate_bias"][layer].rearrange("k h -> h k"),
                                     allow_slow_non_contiguous=True
                                     ).then_inc(const_in, 16)
                        for j in range(3):
                            sp.dma_start(conv_w[:, j, :], io["b_conv_w"][layer, j].rearrange("(h c) -> c h", c=P),
                                         allow_slow_non_contiguous=True
                                         ).then_inc(const_in, 16)
                        sp.dma_start(conv_b[:, :], io["b_conv_b"][layer].rearrange("(h c) -> c h", c=P),
                                     allow_slow_non_contiguous=True
                                     ).then_inc(const_in, 16)
                        sp.dma_start(lam_c[:, :], io["t_lam"][layer]).then_inc(const_in, 16)

                    for c, (kind, subs) in enumerate(CHUNKS):
                        if c == 2:
                            small_loads()
                        if c == 3:
                            sp.dma_start(x_save.rearrange("(t p) d -> p t d", p=P), x).then_inc(x_saved, 16)
                        for j, (src, k0, nk, col, w) in enumerate(subs):
                            n = FIRST_SUB[c] + j
                            if n >= RAW:
                                sp.wait_ge(w_lo, n - RAW + 1)
                            sp.dma_start(wraw[:, n % RAW, 0:nk * w].rearrange("p (k n) -> p k n", k=nk),
                                         w_of[src][layer, :, k0:k0 + nk, col:col + w]
                                         ).then_inc(w_in_s[n % RAW], 16)

                    def sp_in(i, a0, base, par, kind):
                        for j in range(4):
                            r = (base + j) % RAW
                            sp.wait_ge(w_lo, 12 * i + (base + j - RAW + 1))
                            sp.dma_start(wraw[:, r, :].rearrange("p (k n) -> p k n", k=KD),
                                         w_gu[layer, j % 2, 2 * (2 * i + a0) + j // 2]).then_inc(w_in_s[r], 16)

                    def sp_out(i, a0, base, par, kind):
                        for j in range(2):
                            r = (base + j) % RAW
                            sp.wait_ge(w_lo, 12 * i + (base + j - RAW + 1))
                            sp.dma_start(wraw[:, r, :], w_dn[layer, 2 * (2 * i + a0) + j]).then_inc(w_in_s[r], 16)

                    ffn(sp_in, sp_out, sp)
                    sp.wait_ge(x_saved, 16)

                @block.gpsimd
                def _(pool):
                    def wait_stage(m):
                        for i in range(2):
                            cnt = (m + 2 - i) // 2
                            if cnt:
                                pool.wait_ge(stored[i], 16 * cnt)

                    def store_staged(step):
                        m = STAGE[step]
                        s = m % 2
                        if step[0] == "branch":
                            _, b, d = step
                            if m + 1 < len(STAGED):
                                load_gate(m + 1)
                            if b == 2:
                                load_part(d)
                                return
                            pool.wait_ge(mixed, 8 * b + d + 1)
                            if b:
                                pool.wait_ge(stored[s], 16 * ((m - KD) // 2 + 1))
                            add = {"accum_op": ALU.add} if b else {}
                            pool.dma_start(mix_t[d * P:(d + 1) * P, :], stage[:, s, :], **add
                                           ).then_inc(stored[s], 16)
                            return
                        if step in HEADS:
                            pool.wait_ge(h_ready, HEADS[step] + 1)
                        else:
                            pool.wait_ge(act_staged, PLAIN[step] + 1)
                        if step[0] == "bg":
                            dst, src = gates_b, stage[0:16, s, :]
                        elif step[0] == "gate":
                            dst, src = gate_t[step[1], step[2] * P:(step[2] + 1) * P, :], stage[:, s, :]
                        elif step[0] == "bc":
                            dst = conv_in[step[1] * P:(step[1] + 1) * P, :]
                            src = stage[:, s, :]
                        else:
                            c, t = step[1:]
                            rows = slice(t * P, (t + 1) * P)
                            if c < 9:
                                dst, src = qkv_a[rows, c % 3, c // 3, :], stage[:, s, 0:A_W]
                            elif c < C_C:
                                dst = b_vo[rows, c - C_BVO].rearrange("p h e -> p (h e)")
                                src = stage[:, s, 0:B_W]
                            else:
                                dst, src = qkv_c[rows, c - C_C, :], stage[:, s, 0:C_W]
                        pool.dma_start(dst, src).then_inc(stored[s], 16)
                        if step == ("gate", 2, KD - 1):
                            wait_stage(m)
                            load_gate(m + 1)

                    def load_gate(m):
                        _, b, d = STAGED[m]
                        if b == 2 and d >= 2:
                            pool.wait_ge(mixed, 8 * b + d - 1)
                        else:
                            pool.wait_ge(stored[m % 2], 16 * (m // 2))
                        pool.dma_start(stage[:, m % 2, :], gate_t[b, d * P:(d + 1) * P, :]
                                       ).then_inc(gate_in[m % 2], 16)

                    def load_part(d):
                        if d == 0:
                            wait_stage(STORES - 1)
                        if d >= 2:
                            pool.wait_ge(mixed, 16 + d - 1)
                        pool.dma_start(part_mix[:, d % 2, :], mix_t[d * P:(d + 1) * P, :]
                                       ).then_inc(part_in[d % 2], 16)

                    loads = [0, 0, 0]

                    def load_prep(p):
                        g, s, tq, tk = PREPS[p]
                        r = p % 3
                        if p == 0:
                            pool.wait_ge(n_xn, NT)
                            pool.wait_ge(x_saved, 16)
                            pool.wait_ge(n_lo, NT)
                        if p >= 3:
                            pool.wait_ge(a_tr, p - 2)
                            pool.wait_ge(a_pv, LAST_USE[p - 3])
                        if p % len(PREPS) == 0 or PREPS[p - 1][0] != g:
                            wait_stage(STAGE["piece", 3 * g + 2, NT - 1])
                        kv = token_rows(g, s, tk, g == 0)
                        if g == 0 and kv[0][1] < P:
                            h0 = 0 if kv[0][0] else 64
                            pool.memset(a_in[h0:h0 + 64, r, 1:3, :], 0.0).then_inc(a_edge, 1)
                        if g == 0:
                            if tq is not None:
                                p0, m, row, step = token_rows(g, s, tq, False)[0]
                                pool.dma_start(a_in[:, r, 0, :], qkv_a[row:row + m, 0, 0, :]
                                               ).then_inc(a_loaded[r], 16)
                                loads[r] += 1
                            p0, m, row, step = kv[0]
                            pool.dma_start(a_in[p0:p0 + m, r, 1:3, :], qkv_a[row:row + m, 1:3, 0, :]
                                           ).then_inc(a_loaded[r], 16)
                            loads[r] += 1
                        else:
                            for p0, m, row, step in kv:
                                pool.dma_start(a_in[p0:p0 + m, r, :, :],
                                               qkv_a[row:row + step * (m - 1) + 1:step, :, g, :]
                                               ).then_inc(a_loaded[r], 16)
                                loads[r] += 1

                    def store_unit(u):
                        g, s, t, _ = UNITS[u]
                        pool.wait_ge(a_ov, u + 1)
                        for p0, m, row, step in token_rows(g, s, t, False):
                            pool.dma_start(parts_a[row:row + step * (m - 1) + 1:step, g, :], a_o[p0:p0 + m, u % 2, :]
                                           ).then_inc(a_stored[u % 2], 16)

                    def load_merge(t):
                        if t == 0:
                            for i in range(2):
                                pool.wait_ge(a_stored[i], 16 * A_STORES[-1][i])
                        if t >= 2:
                            pool.wait_ge(m_out, t - 1)
                        pool.dma_start(m_in[:, t % 2, :, :], parts_a[t * P:(t + 1) * P, :, :]
                                       ).then_inc(m_loaded[t % 2], 16)

                    def load_conv(u):
                        s, h = B_UNITS[u]
                        t0, n = SEQS[s]
                        if u:
                            pool.wait_ge(b_conv, u)
                        pool.dma_start(b_c[:, 1:1 + n * P], conv_in[h * P:(h + 1) * P, t0 * P:(t0 + n) * P]
                                       ).then_inc(b_cin, 16)

                    def load_vo(u):
                        s, h = B_UNITS[u]
                        t0, n = SEQS[s]
                        rows = slice(t0 * P, (t0 + n) * P)
                        pool.dma_start(b_v[:, 0:n, 0:P], b_vo[rows, 0, h, :].rearrange("(t p) e -> p t e", p=P)
                                       ).then_inc(b_vin, 16)
                        pool.dma_start(b_og[:, 0:n, :], b_vo[rows, 1, h, :].rearrange("(t p) e -> p t e", p=P)
                                       ).then_inc(b_vin, 16)

                    def load_c(p):
                        s, t = C_PREPS[p]
                        t0, n = SEQS[s]
                        rows = slice((t0 + t) * P, (t0 + t + 1) * P)
                        if p == 0:
                            pool.wait_ge(b_store, 16 * len(B_UNITS))
                            pool.dma_start(c_e[:, 0, 0:4 * HD], io["c_lambda"][layer].rearrange("a b -> (a b)")
                                           .partition_broadcast(P)).then_inc(c_lamin, 16)
                        else:
                            pool.wait_ge(c_tr, p)
                        if t == 0 and s == 1:
                            pool.wait_ge(c_pv, SEQS[0][1] * C_H)
                        pool.dma_start(c_in.rearrange("p (i n) -> p i n", i=2), qkv_c[rows, 0:2, :]
                                       ).then_inc(c_lin, 16)
                        pool.dma_start(c_v[:, t, :], qkv_c[rows, 2, :]).then_inc(c_vin, 16)

                    def load_turn(b, t):
                        if b == 1 and t == 0:
                            pool.wait_ge(b_store, 16 * len(B_UNITS))
                        if b == 2:
                            pool.wait_ge(c_store, 16 * (t + 1))
                        if b == 2 or t >= 2:
                            before = ("turn", b, t - 2) if t >= 2 else ("turn", 1, t + NT - 2)
                            pool.wait_ge(d_done, INDEX[before] + 1)
                        src = o_tok[b - 1, t * P:(t + 1) * P, :]
                        pool.dma_start(turn_in[:, t % 2, :], src).then_inc(t_in[t % 2], 16)

                    for step in STEPS:
                        kind = step[0]
                        if step in STAGE:
                            store_staged(step)
                        if kind == "a_load":
                            load_prep(step[1])
                        elif kind == "a_out":
                            store_unit(step[1])
                        elif kind == "a_merge":
                            if step[1] == 0:
                                load_merge(0)
                            if step[1] + 1 < NT:
                                load_merge(step[1] + 1)
                        elif kind == "b_rows":
                            pool.wait_ge(d_done, INDEX["turn", 0, NT - 1] + 1)
                            wait_stage(STAGE["bg",])
                            for d in range(2):
                                pool.dma_start(g_li[0:4, d, :], gates_b[8 * d:8 * d + 4, :]).then_inc(bg_in, 16)
                                pool.dma_start(g_lf[0:4, d, :], gates_b[8 * d + 4:8 * d + 8, :]).then_inc(bg_in, 16)
                        elif kind == "b_columns":
                            pool.wait_ge(bg_cols, 2)
                            pool.dma_start(b_w[:, 0, :, :], io["b_wq"][layer].rearrange("h d e -> d h e")
                                           ).then_inc(b_win, 16)
                            pool.dma_start(b_w[:, 1, :, :], io["b_wk"][layer].rearrange("h d e -> d h e")
                                           ).then_inc(b_win, 16)
                            pool.dma_start(b_hg, io["b_hn_g"][layer].partition_broadcast(P)).then_inc(b_win, 16)
                            wait_stage(STAGE["piece", C_C - 1, NT - 1])
                            load_conv(0)
                            load_vo(0)
                        elif kind == "b_conv" and step[1] + 1 < len(B_UNITS):
                            load_conv(step[1] + 1)
                        elif kind == "b_out":
                            u = step[1]
                            s, h = B_UNITS[u]
                            t0, n = SEQS[s]
                            pool.wait_ge(b_fin, u + 1)
                            pool.dma_start(o_tok[0, t0 * P:(t0 + n) * P, h * P:(h + 1) * P].rearrange(
                                "(t p) e -> p t e", p=P), b_o[:, 0:n, :]).then_inc(b_store, 16)
                            if u + 1 < len(B_UNITS):
                                load_vo(u + 1)
                        elif kind == "c_lambda":
                            wait_stage(STAGE["piece", C_GATE - 1, NT - 1])
                            load_c(0)
                        elif kind == "c_fold":
                            p = step[1]
                            if p + 1 < NT and C_PREPS[p + 1][0] == C_PREPS[p][0]:
                                load_c(p + 1)
                        elif kind == "c_norm":
                            p = step[1]
                            s, t = C_PREPS[p]
                            r0 = (SEQS[s][0] + t) * P
                            pool.wait_ge(co_n, p + 1)
                            pool.dma_start(o_tok[1, r0:r0 + P, :], c_o).then_inc(c_store, 16)
                            if p == SEQS[0][1] - 1:
                                load_c(p + 1)
                        elif kind == "turn_load":
                            load_turn(*step[1:])
                        elif kind == "branch" and step[1] == 2 and 1 <= step[2] <= NT:
                            t = step[2] - 1
                            pool.dma_start(x[:, t, :], x_save[t * P:(t + 1) * P, :]).then_inc(x_back, 16)
                        elif step == ("branch", 2, 0):
                            pool.wait_ge(d_done, INDEX["turn", 2, NT - 1] + 1)
                            pool.dma_start(wide[:, :], io["norm2_g"][layer].partition_broadcast(P)
                                           ).then_inc(gain2_in, 16)

                    for sem_, total in [(a_loaded[i], loads[i]) for i in range(3)] + [
                            (m_loaded[0], NT // 2), (m_loaded[1], NT // 2), (bg_in, 4),
                            (b_cin, len(B_UNITS)), (b_win, 3), (b_vin, 2 * len(B_UNITS)), (b_store, len(B_UNITS)),
                            (c_lamin, 1), (c_lin, NT), (c_vin, NT), (c_store, NT), (t_in[0], NT), (t_in[1], NT),
                            (gain2_in, 1), (x_back, NT), (gate_in[0], 12), (gate_in[1], 12), (part_in[0], 4),
                            (part_in[1], 4)]:
                        pool.wait_ge(sem_, 16 * total)

                @block.scalar
                def _(act):
                    chain = Tally(act, act_c)
                    nc.scalar.preload_act_table_set("natural_log_exp_and_others")

                    def split(c, n):
                        half, j = c % 2, n - FIRST_SUB[c]
                        w = CHUNKS[c][1][j][2] * CHUNKS[c][1][j][4]
                        act.wait_ge(w_in_s[n % RAW], 16 * (n // RAW + 1))
                        if c >= 2:
                            act.wait_ge(d_done, DONE_AT[c - 2])
                        act.activation(wh[:, half, j, 0:w], wraw[:, n % RAW, 0:w], ACT.Copy).then_inc(w_hi, 1)

                    def rstd(out, ss, n):
                        chain.link(act.activation(out, ss, ACT.Ln, scale=1.0 / n, bias=eps[:, 0:1]))
                        return act.activation(out, out, ACT.Exp, scale=-0.5)

                    def sigmoid(x, src):
                        chain.link(act.activation(x, src, ACT.Exp, scale=-1.0))
                        chain.link(act.activation(x, x, ACT.Ln, bias=1.0))
                        return act.activation(x, x, ACT.Exp, scale=-1.0)

                    def rms(m):
                        t = m % NT
                        if m >= NT:
                            act.wait_ge(x_new, WOUT.index((t, 1)) + 1)
                        if m >= 2:
                            act.wait_ge(n_xn, m - 1)
                        s = norm_s[:, m % 2, :]
                        chain.link(act.activation(x_sq, x[:, t, :], ACT.Square, accum_out=s[:, 0:1]))
                        rstd(s[:, 1:2], s[:, 0:1], D).then_inc(n_rstd, 1)

                    def norm(m):
                        t = m % NT
                        act.wait_ge(n_tr, m + 1)
                        act.activation(xh[:, :, t * P:(t + 1) * P],
                                       side[:, 1024 * (m % 2):1024 * (m % 2) + 1024].rearrange("p (k n) -> p k n", k=KD),
                                       ACT.Copy).then_inc(n_hi, 1)

                    def stage_slot(step):
                        m = STAGE[step]
                        if m >= 2:
                            act.wait_ge(stored[m % 2], 16 * (m // 2))
                        return stage[:, m % 2, :]

                    def dense(step):
                        n = INDEX[step]
                        kind = step[0]
                        if step in HEADS:
                            w, i = (A_W if step[1] < 9 else 512), HEADS[step]
                            act.wait_ge(d_done, n + 1)
                            act.activation(ps_pair(n)[:, 1, 0:w], ps_pair(n)[:, 0, 0:w], ACT.Square).then_inc(h_sq, 1)
                            act.wait_ge(h_ss, i + 1)
                            rstd(head_s[:, 1, 0:w // HD], head_s[:, 0, 0:w // HD], HD).then_inc(h_rstd, 1)
                        elif kind == "piece":
                            w = A_W if step[1] < 9 else 512
                            dst = stage_slot(step)[:, 0:w]
                            act.wait_ge(d_done, n + 1)
                            act.activation(dst, ps_pair(n)[:, 0, 0:w], ACT.Copy).then_inc(act_staged, 1)
                        elif kind == "bc":
                            dst = stage_slot(step).rearrange("p (h n) -> p h n", h=2)
                            act.wait_ge(d_done, n + 1)
                            act.activation(dst, ps_pair(n)[:, :, 0:HALF_TOK], ACT.Copy).then_inc(act_staged, 1)
                        elif kind == "bg":
                            dst = stage_slot(step)[0:16, :].rearrange("p (h n) -> p h n", h=2)
                            act.wait_ge(d_done, n + 1)
                            act.activation(dst, ps_pair(n)[0:16, :, 0:HALF_TOK], ACT.Copy).then_inc(act_staged, 1)
                        elif kind == "gate":
                            dst = stage_slot(step).rearrange("p (h n) -> p h n", h=2)
                            act.wait_ge(d_done, n + 1)
                            sigmoid(dst, ps_pair(n)[:, :, 0:HALF_TOK]).then_inc(act_staged, 1)
                        elif kind == "branch" and step[1] == 2:
                            d = step[2]
                            act.wait_ge(mixed, 16 + d + 1)
                            act.activation(xh[:, d, :], mix_raw[:, d % 2, :], ACT.Copy).then_inc(r_hi, 1)
                        elif kind == "turn":
                            _, b, t = step
                            k = MIX_ROWS[b][1]
                            act.wait_ge(d_done, n + 1)
                            act.activation((xh if b == 1 else oh)[:, 0:k, t * P:(t + 1) * P],
                                           ps_pair(n)[:, 0, 0:k * P].rearrange("p (k n) -> p k n", k=k),
                                           ACT.Copy).then_inc(t_hi, 1)

                    def side_step(step):
                        kind = step[0]
                        if kind == "a_fold":
                            p = step[1]
                            r = p % 3
                            act.wait_ge(a_tr, p + 1)
                            if p >= 3:
                                act.wait_ge(a_pv, LAST_USE[p - 3])
                            act.activation(a_qk[:, r, :, :].rearrange("p i n -> p (i n)"), side[:, 0:2 * A_W],
                                           ACT.Copy).then_inc(a_qkt, 1)
                        elif kind == "a_score":
                            u = step[1]
                            nk = len(UNITS[u][3])
                            for h in range(A_H):
                                if h % (A_H // 2) == 0:
                                    act.wait_ge(a_mx, 2 * u + 1 + h // (A_H // 2))
                                pr = a_p[:, h * nk * P:(h + 1) * nk * P]
                                ins = act.activation(pr, pr, ACT.Exp, bias=unit_s[:, h:h + 1], scale=HD ** -0.5,
                                                     accum_out=a_o[:, u % 2, A_W + A_H + h:A_W + A_H + h + 1])
                            ins.then_inc(a_pr, 1)
                        elif kind == "a_turn":
                            u = step[1]
                            nk = len(UNITS[u][3])
                            act.wait_ge(a_ptr, u + 1)
                            at = turned(nk)
                            act.activation(a_pt[:, 0:512 * nk], side[:, at:at + 512 * nk], ACT.Copy).then_inc(a_pta, 1)
                        elif kind == "a_merge":
                            t = step[1]
                            act.wait_ge(m_dif, t + 1)
                            act.activation(m_w[:, 0:18], m_w[:, 0:18], ACT.Exp, scale=HD ** -0.5).then_inc(m_exp, 1)
                        elif kind == "b_gates":
                            act.wait_ge(bg_abs, 1)
                            chain.link(act.activation(g_f[0:4, :, :], g_f[0:4, :, :], ACT.Exp, scale=-1.0))
                            act.activation(g_f[0:4, :, :], g_f[0:4, :, :], ACT.Ln, bias=1.0).then_inc(bg_ln, 1)
                        elif kind == "b_columns":
                            act.wait_ge(bg_col, 1)
                            act.activation(b_g.rearrange("p d t h -> p (d t h)"), side[:, 0:48], ACT.Copy
                                           ).then_inc(bg_cols, 1)
                            act.activation(b_fl.rearrange("p d t h -> p (d t h)"), side[:, 48:96], ACT.Exp,
                                           scale=-1.0).then_inc(bg_cols, 1)
                        elif kind == "b_conv":
                            u = step[1]
                            n = SEQS[B_UNITS[u][0]][1]
                            act.wait_ge(b_conv, u + 1)
                            sigmoid(b_t[:, 0:n * P], b_u[:, 0:n * P]).then_inc(b_exp, 1)
                        elif kind == "b_score":
                            u = step[1]
                            n = SEQS[B_UNITS[u][0]][1]
                            act.wait_ge(b_vin, 32 * (u + 1))
                            sigmoid(b_og[:, 0:n, :], b_og[:, 0:n, :]).then_inc(b_oge, 1)
                        elif kind == "b_qk":
                            u = step[1]
                            n = SEQS[B_UNITS[u][0]][1]
                            act.wait_ge(b_qk, u + 1)
                            act.activation(b_q[:, 0:n * P], side[:, 0:n * P], ACT.Copy).then_inc(b_qke, 1)
                            act.activation(b_k[:, 0:n * P], side[:, 512:512 + n * P], ACT.Copy, scale=P ** -0.5
                                           ).then_inc(b_qke, 1)
                        elif kind == "b_decay":
                            u = step[1]
                            s, h = B_UNITS[u]
                            t0, n = SEQS[s]
                            act.wait_ge(b_dg, u + 1)
                            for d in range(2):
                                for j in range(n):
                                    g = b_g[:, d, t0 + j, h:h + 1]
                                    dm, diag = decay(n, d, j)
                                    bank = side[:, 512 * (2 + d):512 * (2 + d) + 512]
                                    ins = act.activation(diag, diag, ACT.Exp, bias=g)
                                    if d == 0 and j + 1 < n:
                                        ins = act.activation(dm[:, P:], bank[:, (j + 1) * P:n * P], ACT.Exp, bias=g)
                                    if d == 1 and j > 0:
                                        ins = act.activation(dm[:, 0:j * P], bank[:, 0:j * P], ACT.Exp, bias=g)
                            ins.then_inc(b_dec, 1)
                        elif kind == "b_out":
                            u = step[1]
                            n = SEQS[B_UNITS[u][0]][1]
                            act.wait_ge(b_h, u + 1)
                            act.activation(b_t[:, 0:n * P], b_o[:, 0:n, :].rearrange("p t e -> p (t e)"), ACT.Square
                                           ).then_inc(b_sq, 1)
                            act.wait_ge(b_ssq, u + 1)
                            rstd(unit_s[:, 20:20 + n], unit_s[:, 16:16 + n], P).then_inc(b_rs, 1)
                        elif kind == "c_lambda":
                            act.wait_ge(c_lam, 1)
                            act.activation(lam[:, 2:4], lam[:, 0:2], ACT.Exp).then_inc(c_lam, 1)
                        elif kind == "c_fold":
                            p = step[1]
                            s, t = C_PREPS[p]
                            act.wait_ge(c_tr, p + 1)
                            act.activation(c_qt[:, :, t * P:(t + 1) * P], side[:, 0:512].rearrange(
                                "p (h n) -> p h n", h=C_H), ACT.Copy).then_inc(c_qkt, 1)
                            act.activation(c_kt[:, :, t * P:(t + 1) * P], side[:, 512:1024].rearrange(
                                "p (h n) -> p h n", h=C_H), ACT.Copy).then_inc(c_qkt, 1)
                        elif kind == "c_score":
                            u = step[1]
                            n = SEQS[C_UNITS[u][0]][1]
                            act.wait_ge(c_mx, u + 1)
                            if u:
                                act.wait_ge(c_ptr, u)
                            for m in range(2):
                                act.activation(c_e[:, m, 0:n * P], side[:, 512 * m:512 * m + n * P], ACT.Exp,
                                               bias=unit_s[:, 34 + m:35 + m], scale=HD ** -0.5,
                                               accum_out=unit_s[:, 36 + m:37 + m]).then_inc(c_ex, 1)
                        elif kind == "c_turn":
                            u = step[1]
                            n = SEQS[C_UNITS[u][0]][1]
                            act.wait_ge(c_ptr, u + 1)
                            if u:
                                act.wait_ge(c_pv, u)
                            act.activation(c_at[:, 0:n * P], side[:, 1024:1024 + n * P], ACT.Copy).then_inc(c_pt, 1)
                        elif kind == "c_norm":
                            p = step[1]
                            act.wait_ge(c_ov, C_H * (p + 1))
                            act.activation(c_tmp[:, 0:C_W], c_o, ACT.Square).then_inc(co_sq, 1)
                            act.wait_ge(co_ss, p + 1)
                            rstd(unit_s[:, 52:56], unit_s[:, 48:52], P).then_inc(co_rs, 1)
                        elif kind == "ffn_split":
                            act.wait_ge(d_done, INDEX["wout", NT - 1, 0] + 1)
                            for j in range(4):
                                f_split(0, FFN_SUB0 + j, 0, j)

                    def f_split(i, base, half, j):
                        act.wait_ge(w_in_s[base % RAW], 64 * i + 16 * (base // RAW + 1))
                        act.activation(wh[:, half, j, :], wraw[:, base % RAW, :], ACT.Copy).then_inc(w_hi, 1)

                    for step in STEPS:
                        if step[0] == "rms":
                            rms(step[1])
                        elif step[0] == "norm":
                            norm(step[1])
                        elif step[0] == "first":
                            split(step[1] // 4, step[1])
                        elif step in INDEX:
                            dense(step)
                            for c, n in SPLITS.get(step, []):
                                split(c, n)
                        else:
                            side_step(step)

                    nc.scalar.preload_act_table_set("exp_and_others")

                    def silu(i, a0, par, ft):
                        act.wait_ge(f_in, 4 * i + (2 * a0 + ft + 1))
                        act.activation(f_e[:, ft, :].rearrange("p (h n) -> p h n", h=2),
                                       ps[:, 4 * ft:4 * ft + 2, 0:HALF_TOK], ACT.Tanh, scale=0.5).then_inc(f_ex, 1)
                        act.wait_ge(f_hf, 4 * i + (2 * a0 + ft + 1))
                        act.activation(oh[:, 2 * par + ft, :], f_h[:, ft, :], ACT.Copy, scale=0.5).then_inc(f_hi, 1)

                    def act_in(i, a0, base, par, kind):
                        if kind == "first":
                            for ft in range(2):
                                silu(i, a0, par, ft)
                                for j in range(2 * ft, 2 * ft + 2):
                                    f_split(i, base + 4 + j, 0, j)
                            return
                        if kind != "second":
                            act.wait_ge(f_out, 24 * i + 12 * (a0 - 1))
                        for j in range(2):
                            f_split(i, base + 4 + j, 1, j)
                        for ft in range(2):
                            silu(i, a0, par, ft)

                    def act_out(i, a0, base, par, kind):
                        if kind == "last":
                            return
                        act.wait_ge(f_in, 4 * i + min(2 * (a0 + 2), 2 * GROUPS))
                        for j in range(4 if kind == "body" else 2):
                            f_split(i, base + 2 + j, 0, j)

                    ffn(act_in, act_out, act)

                @block.vector
                def _(dve):
                    chain = Tally(dve, dve_c)
                    fch = Tally(dve, f_ch)

                    def split(c, n):
                        half, j = c % 2, n - FIRST_SUB[c]
                        w = CHUNKS[c][1][j][2] * CHUNKS[c][1][j][4]
                        dve.wait_ge(w_hi, n + 1)
                        dve.tensor_tensor(wl[:, half, j, 0:w], wraw[:, n % RAW, 0:w],
                                          wh[:, half, j, 0:w].bitcast(F32), ALU.subtract).then_inc(w_lo, 1)

                    def rms(m):
                        t = m % NT
                        dve.wait_ge(n_rstd, m + 1)
                        if m == 0 or m == NT:
                            dve.wait_ge(gain1_in if m == 0 else gain2_in, 16)
                        if m >= 2:
                            dve.wait_ge(n_tr, m - 1)
                        dve.scalar_tensor_tensor(xn[:, m % 2, :], x[:, t, :], norm_s[:, m % 2, 1:2], wide[:, :],
                                                 ALU.mult, ALU.mult).then_inc(n_xn, 1)

                    def norm(m):
                        t = m % NT
                        dve.wait_ge(n_hi, m + 1)
                        blk = side[:, 1024 * (m % 2):1024 * (m % 2) + 1024].rearrange("p (k n) -> p k n", k=KD)
                        dve.tensor_tensor(xl[:, :, t * P:(t + 1) * P], blk, xh[:, :, t * P:(t + 1) * P].bitcast(F32),
                                          ALU.subtract).then_inc(n_lo, 1)

                    def normed_heads(step, pair):
                        _, c, t = step
                        i, m = HEADS[step], STAGE[step]
                        w, gain, q_k = (A_W, a_gain, c % 3) if c < 9 else (C_W, c_gain, c - C_C)
                        n = w // HD
                        heads = lambda ap: ap.rearrange("p (h c) -> p h c", c=HD)
                        dst, tab = heads(stage[:, m % 2, 0:w]), rope[:, t if t < SEQS[1][0] else t - SEQS[1][0], :]
                        dve.wait_ge(h_sq, i + 1)
                        dve.tensor_reduce(head_s[:, 0, 0:n], heads(pair[:, 1, 0:w]), AX_X, ALU.add).then_inc(h_ss, 1)
                        if i == 0:
                            dve.wait_ge(a_gain_in, 32)
                        if i == 2 * NT:
                            dve.wait_ge(const_in, 16 * 9)
                        if m >= 2:
                            dve.wait_ge(stored[m % 2], 16 * (m // 2))
                        dve.wait_ge(h_rstd, i + 1)
                        dve.tensor_tensor(dst, heads(pair[:, 0, 0:w]), head_s[:, 1, 0:n].unsqueeze(2).to_broadcast(
                            [P, n, HD]), ALU.mult).then_inc(h_scaled, 1)
                        dve.wait_ge(h_scaled, i + 1)
                        chain.link(dve.tensor_tensor(dst, dst, gain[:, q_k, :].unsqueeze(1).to_broadcast([P, n, HD]),
                                                     ALU.mult))
                        x12 = dst[:, :, 0:2 * ROT].rearrange("p h (i c) -> p h i c", i=2)
                        for k in range(2):
                            chain(dve.tensor_tensor(rot[:, k, 0:n], x12, tab[:, k * ROT:(k + 1) * ROT].unsqueeze(1).unsqueeze(
                                1).to_broadcast([P, n, 2, ROT]), ALU.mult))
                        chain.wait()
                        chain(dve.tensor_tensor(dst[:, :, 0:ROT], rot[:, 0, 0:n, 0, :], rot[:, 1, 0:n, 1, :],
                                                ALU.subtract))
                        dve.tensor_tensor(dst[:, :, ROT:2 * ROT], rot[:, 0, 0:n, 1, :], rot[:, 1, 0:n, 0, :], ALU.add
                                          ).then_inc(h_ready, 1)

                    def rest_of_mix(d):
                        dve.wait_ge(r_hi, d + 1)
                        dve.tensor_tensor(xl[:, d, :], mix_raw[:, d % 2, :], xh[:, d, :].bitcast(F32), ALU.subtract
                                          ).then_inc(r_lo, 1)

                    def dense(step):
                        n = INDEX[step]
                        kind = step[0]
                        if step in HEADS:
                            normed_heads(step, ps_pair(n))
                        elif kind == "branch":
                            _, b, d = step
                            i = 8 * b + d
                            m = STAGE[step]
                            e = stage[:, m % 2, :]
                            e2 = e.rearrange("p (h n) -> p h n", h=2)
                            dve.wait_ge(gate_in[m % 2], 16 * (i // 2 + 1))
                            dve.wait_ge(d_done, n + 1)
                            ins = dve.tensor_tensor(e2, ps_pair(n)[:, :, 0:HALF_TOK], e2, ALU.mult)
                            if b < 2:
                                ins.then_inc(mixed, 1)
                            else:
                                chain.link(ins)
                                dve.wait_ge(part_in[d % 2], 16 * (d // 2 + 1))
                                if d >= 2:
                                    dve.wait_ge(r_lo, d - 1)
                                dve.tensor_tensor(mix_raw[:, d % 2, :], e, part_mix[:, d % 2, :], ALU.add
                                                  ).then_inc(mixed, 1)
                                if d:
                                    rest_of_mix(d - 1)
                                if d == KD - 1:
                                    rest_of_mix(d)
                        elif kind == "turn":
                            _, b, t = step
                            k = MIX_ROWS[b][1]
                            dve.wait_ge(t_hi, NT * b + t + 1)
                            hi, lo = (xh, xl) if b == 1 else (oh, ol)
                            dve.tensor_tensor(lo[:, 0:k, t * P:(t + 1) * P],
                                              ps_pair(n)[:, 0, 0:k * P].rearrange("p (k n) -> p k n", k=k),
                                              hi[:, 0:k, t * P:(t + 1) * P].bitcast(F32), ALU.subtract
                                              ).then_inc(t_lo, 1)
                        elif kind == "wout":
                            _, t, h = step
                            if (t, h) == WOUT[0]:
                                dve.wait_ge(x_back, 16 * NT)
                            dve.wait_ge(d_done, n + 1)
                            xx = x[:, t, h * 512:(h + 1) * 512]
                            dve.tensor_tensor(xx, ps_pair(n)[:, 0, :], xx, ALU.add).then_inc(x_new, 1)

                    def side_step(step):
                        kind = step[0]
                        if kind == "a_score":
                            u = step[1]
                            g, s, t, pr = UNITS[u]
                            nk = len(pr)
                            dve.wait_ge(a_sc, u + 1)
                            if u >= 1:
                                dve.wait_ge(a_ptr, u)
                            if u >= 2:
                                dve.wait_ge(a_stored[u % 2], 16 * A_STORES[u - 2][u % 2])
                            mk = masks[:, mask_of(g, s, t), :]
                            for h in range(A_H):
                                if h == A_H // 2:
                                    chain.wait()
                                    dve.tensor_scalar(unit_s[:, 0:h], a_o[:, u % 2, A_W:A_W + h], -HD ** -0.5, None,
                                                      ALU.mult).then_inc(a_mx, 1)
                                sl = slice(h * nk * P, (h + 1) * nk * P)
                                chain(dve.tensor_tensor_reduce(
                                    a_p[:, sl].rearrange("p (k n) -> p k n", k=nk),
                                    score_bank(nk, h).rearrange("p (k n) -> p k n", k=nk), mk, 1.0, -3e38, ALU.add, ALU.max,
                                    a_o[:, u % 2, A_W + h:A_W + h + 1]))
                            chain.wait()
                            dve.tensor_scalar(unit_s[:, A_H // 2:A_H], a_o[:, u % 2, A_W + A_H // 2:A_W + A_H],
                                              -HD ** -0.5, None, ALU.mult).then_inc(a_mx, 1)
                        elif kind == "a_turn":
                            u = step[1]
                            nk = len(UNITS[u][3])
                            dve.wait_ge(a_ptr, u + 1)
                            at = turned(nk)
                            dve.tensor_copy(a_pt[:, 512 * nk:768 * nk], side[:, at + 512 * nk:at + 768 * nk]
                                            ).then_inc(a_ptd, 1)
                        elif kind == "a_out":
                            u = step[1]
                            dve.wait_ge(a_pv, u + 1)
                            dve.tensor_copy(a_o[:, u % 2, 0:A_W], side[:, unit_out(u):unit_out(u) + A_W]).then_inc(a_ov, 1)
                        elif kind == "a_merge":
                            t = step[1]
                            dve.wait_ge(m_loaded[t % 2], 16 * (t // 2 + 1))
                            mi = m_in[:, t % 2, :, :]
                            if t >= 2:
                                dve.wait_ge(d_done, INDEX["turn", 0, t - 2] + 1)
                            mxs, den = mi[:, :, A_W:A_W + A_H], mi[:, :, A_W + A_H:]
                            w = m_w[:, 0:18].rearrange("p (g h) -> p g h", g=A_G)
                            top, wd, tot = m_w[:, 18:24], m_w[:, 24:42].rearrange("p (g h) -> p g h", g=A_G), m_w[:, 42:48]
                            chain.link(dve.tensor_tensor(top, mxs[:, 0, :], mxs[:, 1, :], ALU.max))
                            chain.link(dve.tensor_tensor(top, top, mxs[:, 2, :], ALU.max))
                            dve.tensor_tensor(w, mxs, top.unsqueeze(1).to_broadcast([P, A_G, A_H]), ALU.subtract
                                              ).then_inc(m_dif, 1)
                            dve.wait_ge(m_exp, t + 1)
                            chain.link(dve.tensor_tensor(wd, w, den, ALU.mult))
                            chain.link(dve.tensor_tensor(tot, wd[:, 0, :], wd[:, 1, :], ALU.add))
                            chain.link(dve.tensor_tensor(tot, tot, wd[:, 2, :], ALU.add))
                            chain.link(dve.reciprocal(tot, tot))
                            chain.link(dve.tensor_tensor(wd, w, tot.unsqueeze(1).to_broadcast([P, A_G, A_H]), ALU.mult))
                            for g in range(A_G):
                                chain(dve.tensor_tensor(
                                    m_sc[:, g], mi[:, g, 0:A_W].rearrange("p (h c) -> p h c", h=A_H),
                                    wd[:, g, :].unsqueeze(2).to_broadcast([P, A_H, HD]), ALU.mult))
                            chain.wait()
                            chain.link(dve.tensor_tensor(m_sc[:, 0], m_sc[:, 0], m_sc[:, 1], ALU.add))
                            dve.tensor_tensor(m_o[:, t % 2, :].rearrange("p (h c) -> p h c", h=A_H), m_sc[:, 0],
                                              m_sc[:, 2], ALU.add).then_inc(m_out, 1)
                        elif kind == "b_gates":
                            dve.wait_ge(d_done, INDEX["turn", 0, NT - 1] + 1)
                            chain(dve.memset(g_zero, 0.0))
                            dve.wait_ge(bg_in, 64)
                            for d in range(2):
                                for k, v in enumerate((g_li, g_lf)):
                                    chain(dve.tensor_scalar(v[0:4, d, :], v[0:4, d, :], gate_bias[0:4, 2 * d + k:2 * d + k + 1],
                                                            None, ALU.add))
                            chain.wait()
                            dve.scalar_tensor_tensor(g_f[0:4, :, :], g_lf[0:4, :, :], -1.0, g_lf[0:4, :, :], ALU.mult,
                                                     ALU.max).then_inc(bg_abs, 1)
                            chain.link(dve.tensor_scalar(g_lf[0:4, :, :], g_lf[0:4, :, :], 0.0, None, ALU.min))
                        elif kind == "b_scan":
                            if step[1] == 0:
                                dve.wait_ge(bg_ln, 1)
                                chain.link(dve.tensor_tensor(g_lf[0:4, :, :], g_lf[0:4, :, :], g_f[0:4, :, :],
                                                             ALU.subtract))
                            d, (t0, n) = step[1] // 2, SEQS[step[1] % 2]
                            sl = slice(t0 * P, (t0 + n) * P)

                            def in_order(ap):
                                v = ap[0:4, d, sl]
                                return v if d == 0 else v[:, ::-1]

                            li, lf, ff, mx = (in_order(v) for v in (g_li, g_lf, g_f, nmx))
                            chain.link(dve.tensor_tensor_scan(ff, g_zero[0:4, 0:n * P], lf, 0.0, ALU.add, ALU.add))
                            chain.link(dve.tensor_tensor(li, li, ff, ALU.subtract))
                            chain.link(dve.tensor_tensor_scan(mx, li, li, 0.0, ALU.max, ALU.max))
                            chain.link(dve.tensor_tensor(ff, ff, mx, ALU.add))
                            dve.tensor_scalar(mx, mx, -1.0, None, ALU.mult).then_inc(bg_scan, 1)
                        elif kind == "b_conv":
                            u = step[1]
                            s, h = B_UNITS[u]
                            n = SEQS[s][1]
                            S = n * P
                            if u == 0:
                                dve.wait_ge(bg_cols, 2)
                                chain(dve.memset(b_v[:, :, P:P + 1], 1.0))
                            chain(dve.memset(b_c[:, 0:1], 0.0))
                            chain(dve.memset(b_c[:, S + 1:S + 2], 0.0))
                            chain.wait()
                            dve.wait_ge(b_cin, 16 * (u + 1))
                            uu = b_u[:, 0:S]
                            if u:
                                dve.wait_ge(b_qk, u)
                            chain.link(dve.tensor_scalar(uu, b_c[:, 0:S], conv_w[:, 0, h:h + 1], conv_b[:, h:h + 1],
                                                         ALU.mult, ALU.add))
                            chain.link(dve.scalar_tensor_tensor(uu, b_c[:, 1:S + 1], conv_w[:, 1, h:h + 1], uu,
                                                                ALU.mult, ALU.add))
                            dve.scalar_tensor_tensor(uu, b_c[:, 2:S + 2], conv_w[:, 2, h:h + 1], uu, ALU.mult,
                                                     ALU.add).then_inc(b_conv, 1)
                            dve.wait_ge(b_exp, u + 1)
                            dve.tensor_tensor(uu, uu, b_t[:, 0:S], ALU.mult).then_inc(b_u_s, 1)
                        elif kind == "b_decay":
                            u = step[1]
                            s, h = B_UNITS[u]
                            n = SEQS[s][1]
                            dve.wait_ge(b_bc, u + 1)
                            for d in range(2):
                                for j in range(n):
                                    bank = side[:, 512 * (2 + d):512 * (2 + d) + 512]
                                    ins = dve.tensor_tensor(decay(n, d, j)[1], bank[:, j * P:(j + 1) * P],
                                                            masks[:, 1 + d, :], ALU.add)
                            ins.then_inc(b_dg, 1)
                        elif kind == "b_score":
                            u = step[1]
                            s, h = B_UNITS[u]
                            n = SEQS[s][1]
                            dve.wait_ge(b_sc, u + 1)
                            dve.wait_ge(b_dec, u + 1)
                            for j in range(n):
                                f, b = decay(n, 0, j)[0], decay(n, 1, j)[0]
                                dve.tensor_tensor(f, side[:, 512 * j + j * P:512 * j + n * P], f, ALU.mult)
                                ins = dve.tensor_tensor(b, side[:, 512 * j:512 * j + (j + 1) * P], b, ALU.mult)
                            ins.then_inc(b_wt, 1)
                        elif kind == "b_out":
                            u = step[1]
                            s, h = B_UNITS[u]
                            t0, n = SEQS[s]
                            S = n * P
                            dve.wait_ge(b_nd, u + 1)
                            nd = side[:, 0:512 * n].rearrange("p (t d n) -> p t d n", t=n, d=2)
                            r = unit_s[:, 0:2 * n].rearrange("p (t d) -> p t d", t=n)
                            hb = [b_d[:, i, 0:S].rearrange("p (t e) -> p t e", t=n) for i in range(2)]
                            if u:
                                dve.wait_ge(b_store, 16 * u)
                            chain.link(dve.tensor_copy(r, nd[:, :, :, P]))
                            chain.link(dve.scalar_tensor_tensor(r, r, -1.0, r, ALU.mult, ALU.max))
                            chain.link(dve.tensor_tensor(r, r, b_fl[:, :, t0:t0 + n, h].rearrange("p d t -> p t d"),
                                                         ALU.max))
                            chain.link(dve.reciprocal(r, r))
                            for i in range(2):
                                chain(dve.tensor_tensor(hb[i], nd[:, :, i, 0:P], r[:, :, i:i + 1].to_broadcast(
                                    [P, n, P]), ALU.mult))
                            chain.wait()
                            o = b_o[:, 0:n, :]
                            dve.tensor_tensor(o, hb[0], hb[1], ALU.add).then_inc(b_h, 1)
                            dve.wait_ge(b_sq, u + 1)
                            dve.tensor_reduce(unit_s[:, 16:16 + n], b_t[:, 0:S].rearrange("p (t e) -> p t e", t=n),
                                              AX_X, ALU.add).then_inc(b_ssq, 1)
                            dve.wait_ge(b_rs, u + 1)
                            chain.link(dve.tensor_tensor(o, o, unit_s[:, 20:20 + n].unsqueeze(2).to_broadcast([P, n, P]),
                                                         ALU.mult))
                            chain.link(dve.tensor_tensor(o, o, b_hg[:, h * P:(h + 1) * P].unsqueeze(1).to_broadcast(
                                [P, n, P]), ALU.mult))
                            dve.wait_ge(b_oge, u + 1)
                            dve.tensor_tensor(o, o, b_og[:, 0:n, :], ALU.mult).then_inc(b_fin, 1)
                        elif kind == "c_lambda":
                            dve.wait_ge(c_lamin, 16)
                            cl = c_e[:, 0, 0:256].rearrange("p (i c) -> p i c", i=4)
                            for i in range(2):
                                chain(dve.tensor_tensor_reduce(
                                    c_at[:, i * HD:(i + 1) * HD], cl[:, 2 * i, :], cl[:, 2 * i + 1, :], 1.0, 0.0,
                                    ALU.mult, ALU.add, unit_s[:, 60 + i:61 + i]))
                            chain.wait()
                            dve.tensor_copy(lam[:, 0:2], unit_s[:, 60:62]).then_inc(c_lam, 1)
                            dve.wait_ge(c_lam, 2)
                            chain.link(dve.tensor_tensor(lam[:, 0:1], lam[:, 2:3], lam[:, 3:4], ALU.subtract))
                            chain.link(dve.tensor_tensor(lam[:, 0:1], lam[:, 0:1], lam_c[:, 0:1], ALU.add))
                            chain.link(dve.tensor_scalar(c_hgain[:, :], c_hgain[:, :], lam_c[:, 1:2], None, ALU.mult))
                        elif kind == "c_score":
                            u = step[1]
                            n = SEQS[C_UNITS[u][0]][1]
                            dve.wait_ge(c_sc, u + 1)
                            if u:
                                dve.wait_ge(c_ex, 2 * u)
                            chain.link(dve.tensor_reduce(unit_s[:, 32:34], side[:, 0:1024].rearrange(
                                "p (m n) -> p m n", m=2)[:, :, 0:n * P], AX_X, ALU.max))
                            dve.tensor_scalar(unit_s[:, 34:36], unit_s[:, 32:34], -HD ** -0.5, None, ALU.mult
                                              ).then_inc(c_mx, 1)
                            dve.wait_ge(c_ex, 2 * (u + 1))
                            chain.link(dve.reciprocal(unit_s[:, 38:40], unit_s[:, 36:38]))
                            chain.link(dve.tensor_tensor(unit_s[:, 39:40], unit_s[:, 39:40], lam[:, 0:1], ALU.mult))
                            e0, e1 = c_e[:, 0, 0:n * P], c_e[:, 1, 0:n * P]
                            chain.link(dve.tensor_scalar(e1, e1, unit_s[:, 39:40], None, ALU.mult))
                            dve.scalar_tensor_tensor(e0, e0, unit_s[:, 38:39], e1, ALU.mult, ALU.subtract
                                                     ).then_inc(c_a, 1)
                        elif kind == "c_out":
                            u = step[1]
                            s, t, h = C_UNITS[u]
                            dve.wait_ge(c_pv, u + 1)
                            if h == 0 and u:
                                dve.wait_ge(c_store, 16 * (u // C_H))
                            dve.tensor_copy(c_o[:, h * P:(h + 1) * P], side[:, 1536:1536 + P]).then_inc(c_ov, 1)
                        elif kind == "c_norm":
                            p = step[1]
                            dve.wait_ge(co_sq, p + 1)
                            dve.tensor_reduce(unit_s[:, 48:52], c_tmp[:, 0:C_W].rearrange("p (h e) -> p h e", e=P), AX_X,
                                              ALU.add).then_inc(co_ss, 1)
                            dve.wait_ge(co_rs, p + 1)
                            o = c_o.rearrange("p (h e) -> p h e", e=P)
                            chain.link(dve.tensor_tensor(o, o, unit_s[:, 52:56].unsqueeze(2).to_broadcast([P, C_H, P]),
                                                         ALU.mult))
                            dve.tensor_tensor(o, o, c_hgain[:, :].unsqueeze(1).to_broadcast([P, C_H, P]), ALU.mult
                                              ).then_inc(co_n, 1)
                        elif kind == "ffn_split":
                            for j in range(4):
                                f_split(0, FFN_SUB0 + j, 0, j)

                    def f_split(i, base, half, j):
                        dve.wait_ge(w_hi, 12 * i + (base + 1))
                        dve.tensor_tensor(wl[:, half, j, :], wraw[:, base % RAW, :], wh[:, half, j, :].bitcast(F32),
                                          ALU.subtract).then_inc(w_lo, 1)

                    for step in STEPS:
                        if step[0] == "rms":
                            rms(step[1])
                        elif step[0] == "norm":
                            norm(step[1])
                        elif step[0] == "first":
                            split(step[1] // 4, step[1])
                        elif step in INDEX:
                            dense(step)
                            for c, n in SPLITS.get(step, []):
                                split(c, n)
                        else:
                            side_step(step)

                    def silu(i, a0, par, ft):
                        e = f_e[:, ft, :]
                        e2 = e.rearrange("p (h n) -> p h n", h=2)
                        dve.wait_ge(f_ex, 4 * i + (2 * a0 + ft + 1))
                        fch.link(dve.scalar_tensor_tensor(e2, e2, 1.0, ps[:, 4 * ft:4 * ft + 2, 0:HALF_TOK], ALU.add,
                                                          ALU.mult))
                        dve.tensor_tensor(f_h[:, ft, :].rearrange("p (h n) -> p h n", h=2),
                                          ps[:, 4 * ft + 2:4 * ft + 4, 0:HALF_TOK], e2, ALU.mult).then_inc(f_hf, 1)
                        dve.wait_ge(f_hi, 4 * i + (2 * a0 + ft + 1))
                        dve.scalar_tensor_tensor(ol[:, 2 * par + ft, :], f_h[:, ft, :], 0.5,
                                                 oh[:, 2 * par + ft, :].bitcast(F32), ALU.mult, ALU.subtract
                                                 ).then_inc(f_lo, 1)

                    def dve_in(i, a0, base, par, kind):
                        if kind == "first":
                            for ft in range(2):
                                silu(i, a0, par, ft)
                                for j in range(2 * ft, 2 * ft + 2):
                                    f_split(i, base + 4 + j, 0, j)
                            return
                        for j in range(2):
                            f_split(i, base + 4 + j, 1, j)
                        for ft in range(2):
                            silu(i, a0, par, ft)

                    def dve_out(i, a0, base, par, kind):
                        splits = {"body": 4, "before last": 2, "last": 0}[kind]
                        for q in range(12):
                            t, h = q // 2, q % 2
                            xx = x[:, t, h * 512:(h + 1) * 512]
                            dve.wait_ge(f_out, 24 * i + (12 * a0 + q + 1))
                            dve.tensor_tensor(xx, ps[:, q % 8, :], xx, ALU.add).then_inc(f_add, 1)
                            if q % 2 == 1 and q // 2 < splits:
                                f_split(i, base + 2 + q // 2, 0, q // 2)

                    fch.per = 2 * 2
                    ffn(dve_in, dve_out, dve, (fch,))
                    dve.wait_ge(f_add, 12 * GROUPS)

                @block.tensor
                def _(pe):
                    def product(out, ah, al, bh, bl, first, last):
                        pe.matmul(out, ah, bh, start=first, stop=False)
                        pe.matmul(out, ah, bl, start=False, stop=False)
                        return pe.matmul(out, al, bh, start=False, stop=last)

                    def wait_pair(n):
                        if n >= 2:
                            sem_, val = FREED[n - 2]
                            pe.wait_ge(sem_, val)

                    def weights(c, j, k, w):
                        sl = slice(k * w, (k + 1) * w)
                        return wh[:, c % 2, j, sl], wl[:, c % 2, j, sl]

                    def dense(step):
                        n = INDEX[step]
                        pair = ps_pair(n)
                        wait_pair(n)
                        kind = step[0]
                        if kind == "piece" or kind == "wout":
                            if kind == "piece":
                                c, t = step[1:]
                            else:
                                t, c = step[1], C_OUT + step[2]
                                pe.wait_ge(r_lo, KD)
                            w = CHUNKS[c][1][0][4]
                            if c == 0:
                                pe.wait_ge(n_lo, t + 1)
                            for k in range(KD):
                                if t == 0 and k % 2 == 0:
                                    pe.wait_ge(w_lo, FIRST_SUB[c] + k // 2 + 1)
                                th, tl = (v[:, k, t * P:(t + 1) * P] for v in (xh, xl))
                                bh, bl = weights(c, k // 2, k % 2, w)
                                mm = product(pair[:, 0, 0:w], th, tl, bh, bl, k == 0, k == KD - 1)
                            mm.then_inc(d_done, 1)
                        elif kind in ("bc", "bg", "gate", "branch"):
                            c, j = chunk_of(step)
                            src, at, w = (xh, xl), 0, CHUNKS[c][1][j][4]
                            if kind == "branch":
                                src = (xh, xl) if step[1] == 1 else (oh, ol)
                                at = P * (step[2] % 2)
                                pe.wait_ge(t_lo, NT * (step[1] + 1))
                            pe.wait_ge(w_lo, FIRST_SUB[c] + j + 1)
                            mm = wide_product(pair, c % 2, j, CHUNKS[c][1][j][2], w, at, min(w, P), *src)
                            mm.then_inc(d_done, 1)
                        elif kind == "turn":
                            _, b, t = step
                            if b == 0:
                                pe.wait_ge(m_out, t + 1)
                            else:
                                pe.wait_ge(t_in[t % 2], 16 * (3 * (b - 1) + t // 2 + 1))
                            for k in range(MIX_ROWS[b][1]):
                                src = m_o[:, t % 2, k * P:(k + 1) * P] if b == 0 else turn_in[:, t % 2, k * P:(k + 1) * P]
                                mm = pe.transpose(pair[:, 0, k * P:(k + 1) * P], src, ident[:, :])
                            mm.then_inc(d_done, 1)

                    def wide_product(pair, half, j, nk, w_row, at, cols, sh, sl):
                        for k in range(nk):
                            sl_ = slice(k * w_row + at, k * w_row + at + cols)
                            for w, acts in ((wh, (sh, sl)), (wl, (sh,))):
                                for a, v in enumerate(acts):
                                    for q in range(2):
                                        mm = pe.matmul(pair[0:cols, q, 0:HALF_TOK], w[:, half, j, sl_],
                                                       v[:, k, q * HALF_TOK:(q + 1) * HALF_TOK],
                                                       start=(k == 0 and w is wh and a == 0),
                                                       stop=(k == nk - 1 and w is wl))
                        return mm

                    def norm(m):
                        pe.wait_ge(n_xn, m + 1)
                        if m >= 2:
                            pe.wait_ge(n_lo, m - 1)
                        for k in range(KD):
                            at = 1024 * (m % 2) + k * P
                            mm = pe.transpose(side[:, at:at + P], xn[:, m % 2, k * P:(k + 1) * P], ident[:, :])
                        mm.then_inc(n_tr, 1)

                    def side_step(step):
                        kind = step[0]
                        if kind == "a_fold":
                            p = step[1]
                            r = p % 3
                            pe.wait_ge(a_loaded[r], 16 * A_LOADS[p])
                            if A_EDGES[p]:
                                pe.wait_ge(a_edge, A_EDGES[p])
                            before = [k[0] for k in STEPS[:STEPS.index(step)]]
                            u = before.count("a_out")
                            if "a_score" in before:
                                pe.wait_ge(a_mx, 2 * before.count("a_score"))
                            if u:
                                pe.wait_ge(a_pta, u)
                                pe.wait_ge(a_ptd, u)
                            if p:
                                pe.wait_ge(a_qkt, p)
                            for i in range(6):
                                mm = pe.transpose(side[:, i * P:(i + 1) * P],
                                                  a_in[:, r, i // 3, (i % 3) * P:(i % 3 + 1) * P], ident[:, :])
                            mm.then_inc(a_tr, 1)
                        elif kind == "a_score":
                            u = step[1]
                            g, s, t, pr = UNITS[u]
                            pe.wait_ge(a_qkt, pr[-1] + 1)
                            if u and len(pr) == 2:
                                pe.wait_ge(a_ov, u)
                            for h in range(A_H):
                                b = HD * (h % 2)
                                for i, p in enumerate(pr):
                                    mm = pe.matmul(score_bank(len(pr), h)[:, i * P:(i + 1) * P],
                                                   a_qk[b:b + HD, pr[0] % 3, h // 2, :],
                                                   a_qk[b:b + HD, p % 3, 3 + h // 2, :], start=True, stop=True)
                            mm.then_inc(a_sc, 1)
                        elif kind == "a_turn":
                            u = step[1]
                            nk = len(UNITS[u][3])
                            at = turned(nk)
                            pe.wait_ge(a_pr, u + 1)
                            if nk == 1:
                                pe.wait_ge(a_ov, u)
                            for i in range(A_H * nk):
                                mm = pe.transpose(side[:, at + i * P:at + (i + 1) * P], a_p[:, i * P:(i + 1) * P], ident[:, :])
                            mm.then_inc(a_ptr, 1)
                        elif kind == "a_out":
                            u = step[1]
                            g, s, t, pr = UNITS[u]
                            nk = len(pr)
                            pe.wait_ge(a_pta, u + 1)
                            pe.wait_ge(a_ptd, u + 1)
                            for h in range(A_H):
                                for i, p in enumerate(pr):
                                    at = (h * nk + i) * P
                                    o = unit_out(u) + h * HD
                                    mm = pe.matmul(side[:, o:o + HD], a_pt[:, at:at + P],
                                                   a_in[:, p % 3, 2, h * HD:(h + 1) * HD], start=(i == 0),
                                                   stop=(i == nk - 1))
                            mm.then_inc(a_pv, 1)
                        elif kind == "b_columns":
                            pe.wait_ge(bg_scan, 4)
                            for i, src in enumerate((g_li, g_f)):
                                for d in range(2):
                                    for t in range(NT):
                                        at = 48 * i + 24 * d + 4 * t
                                        mm = pe.transpose(side[:, at:at + 4], src[0:4, d, t * P:(t + 1) * P],
                                                          ident[0:4, 0:4])
                            mm.then_inc(bg_col, 1)
                        elif kind == "b_qk":
                            u = step[1]
                            s, h = B_UNITS[u]
                            n = SEQS[s][1]
                            pe.wait_ge(b_u_s, u + 1)
                            if u == 0:
                                pe.wait_ge(b_win, 48)
                                pe.wait_ge(bg_cols, 2)
                            else:
                                pe.wait_ge(b_h, u)
                            for i in range(2):
                                pe_mm = pe.matmul(side[:, 512 * i:512 * i + n * P], b_w[:, i, h, :], b_u[:, 0:n * P],
                                                  start=True, stop=True)
                            pe_mm.then_inc(b_qk, 1)
                        elif kind == "b_decay":
                            u = step[1]
                            s, h = B_UNITS[u]
                            t0, n = SEQS[s]
                            if u:
                                pe.wait_ge(b_h, u)
                            for d in range(2):
                                mm = pe.matmul(side[:, 512 * (2 + d):512 * (2 + d) + n * P],
                                               ident[0:4, h:h + 1].to_broadcast([4, P]),
                                               nmx[0:4, d, t0 * P:(t0 + n) * P], start=True, stop=True)
                            mm.then_inc(b_bc, 1)
                        elif kind == "b_score":
                            u = step[1]
                            s, h = B_UNITS[u]
                            n = SEQS[s][1]
                            pe.wait_ge(b_qke, 2 * (u + 1))
                            pe.wait_ge(b_dec, u + 1)
                            for j in range(n):
                                mm = pe.matmul(side[:, 512 * j:512 * j + n * P], b_k[:, j * P:(j + 1) * P],
                                               b_q[:, 0:n * P], start=True, stop=True)
                            mm.then_inc(b_sc, 1)
                        elif kind == "b_out":
                            u = step[1]
                            s, h = B_UNITS[u]
                            n = SEQS[s][1]
                            pe.wait_ge(b_wt, u + 1)
                            pe.wait_ge(b_vin, 32 * (u + 1))
                            for t in range(n):
                                for d in range(2):
                                    js = list(range(0, t + 1)) if d == 0 else list(range(t, n))
                                    for j in js:
                                        dm = decay(n, d, j)[0]
                                        at = (t - j) * P if d == 0 else t * P
                                        mm = pe.matmul(side[:, 512 * t + 256 * d:512 * t + 256 * d + P + 1],
                                                       dm[:, at:at + P], b_v[:, j, :], start=(j == js[0]),
                                                       stop=(j == js[-1]))
                            mm.then_inc(b_nd, 1)
                        elif kind == "c_fold":
                            p = step[1]
                            pe.wait_ge(c_lin, 16 * (p + 1))
                            if p:
                                pe.wait_ge(c_qkt, 2 * p)
                            if C_PREPS[p] == (1, 0):
                                pe.wait_ge(c_ex, 2 * SEQS[0][1] * C_H)
                            for i in range(8):
                                mm = pe.transpose(side[:, i * P:(i + 1) * P], c_in[:, i * P:(i + 1) * P], ident[:, :])
                            mm.then_inc(c_tr, 1)
                        elif kind == "c_score":
                            u = step[1]
                            s, t, h = C_UNITS[u]
                            n = SEQS[s][1]
                            pe.wait_ge(c_qkt, 2 * (SEQS[s][0] + n))
                            if u:
                                pe.wait_ge(c_ex, 2 * u)
                            for m in range(2):
                                b = HD * m
                                mm = pe.matmul(side[:, 512 * m:512 * m + n * P], c_qt[b:b + HD, h, t * P:(t + 1) * P],
                                               c_kt[b:b + HD, h, 0:n * P], start=True, stop=True)
                            mm.then_inc(c_sc, 1)
                        elif kind == "c_turn":
                            u = step[1]
                            n = SEQS[C_UNITS[u][0]][1]
                            pe.wait_ge(c_a, u + 1)
                            if u:
                                pe.wait_ge(c_pt, u)
                            for i in range(n):
                                mm = pe.transpose(side[:, 1024 + i * P:1024 + (i + 1) * P], c_e[:, 0, i * P:(i + 1) * P],
                                                  ident[:, :])
                            mm.then_inc(c_ptr, 1)
                        elif kind == "c_out":
                            u = step[1]
                            s, t, h = C_UNITS[u]
                            n = SEQS[s][1]
                            pe.wait_ge(c_pt, u + 1)
                            pe.wait_ge(c_vin, 16 * (SEQS[s][0] + n))
                            if u:
                                pe.wait_ge(c_ov, u)
                            for i in range(n):
                                mm = pe.matmul(side[:, 1536:1536 + P], c_at[:, i * P:(i + 1) * P],
                                               c_v[:, i, h * P:(h + 1) * P], start=(i == 0), stop=(i == n - 1))
                            mm.then_inc(c_pv, 1)

                    for step in STEPS:
                        if step[0] == "norm":
                            norm(step[1])
                        elif step in INDEX:
                            dense(step)
                        else:
                            side_step(step)

                    pe.wait_ge(n_lo, 2 * NT)

                    def pe_in(i, a0, base, par, kind):
                        for ft in range(2):
                            if kind == "first":
                                pe.wait_ge(x_new, 2 * NT)
                            elif kind == "second":
                                pe.wait_ge(f_hf, ft + 1)
                            else:
                                pe.wait_ge(f_add, 24 * i + 12 * (a0 - 1))
                            for u in range(2):
                                j = 2 * ft + u
                                pe.wait_ge(w_lo, 12 * i + (base + j + 1))
                                mm = wide_product(ps[:, 4 * ft + 2 * u:4 * ft + 2 * u + 2, :], 0, j, KD, P, 0, P, xh, xl)
                            mm.then_inc(f_in, 1)

                    def pe_out(i, a0, base, par, kind):
                        half = 0 if kind == "last" else 1
                        pe.wait_ge(f_lo, 4 * i + (2 * a0 + 2))
                        for q in range(12):
                            t, h = q // 2, q % 2
                            if q >= 8:
                                pe.wait_ge(f_add, 24 * i + (12 * a0 + q - 7))
                            elif kind == "last" and q < 4:
                                pe.wait_ge(f_add, 12 * a0 + q - 3)
                            elif kind != "last" and q % 4 == 0:
                                pe.wait_ge(f_hf, 4 * i + (2 * a0 + 3 + q // 4))
                            for ft in range(2):
                                if q == 0:
                                    pe.wait_ge(w_lo, 12 * i + (base + ft + 1))
                                th, tl = (v[:, 2 * par + ft, t * P:(t + 1) * P] for v in (oh, ol))
                                bh, bl = (v[:, half, ft, h * 512:(h + 1) * 512] for v in (wh, wl))
                                mm = product(ps[:, q % 8, :], th, tl, bh, bl, ft == 0, ft == 1)
                            mm.then_inc(f_out, 1)

                    ffn(pe_in, pe_out, pe)

            nc.gpsimd.dma_reset()
            first = min(s.num for s in sems)
            assert sorted(s.num for s in sems) == list(range(first, first + len(sems)))
            nc.gpsimd.sem_clear(range(first, first + len(sems)))
            nc.all_engine_barrier()

        with nc.Block() as block:
            @block.sync
            def _(sp):
                sp.dma_start(io["y_prompt"].rearrange("b (t p) d -> p (b t) d", p=P), x[:, 0:2, :]).then_inc(start, 16)
                sp.dma_start(io["y_sample"].rearrange("b (t p) d -> p (b t) d", p=P), x[:, 2:NT, :]
                             ).then_inc(start, 16)
                sp.wait_ge(start, 112)


_INS = ["x_prompt", "x_sample", "norm1_g", "w_in", "a_qn_g", "a_kn_g", "b_conv_w", "b_conv_b", "b_wq", "b_wk",
        "b_gate_bias", "b_hn_g", "c_qn_g", "c_kn_g", "c_lambda", "c_hn_g", "w_branch", "w_out", "norm2_g", "w_ffn_in",
        "w_ffn_out"]
_OUTS = [("y_prompt", (1, 256, D)), ("y_sample", (1, 512, D))]


def kernel(**inputs):
    import numpy as _np
    import concourse.bacc as _bacc
    from concourse import mybir as _mybir
    from concourse.bass_utils import run_bass_kernel_spmd as _run

    nc = _bacc.Bacc("TRN2", target_bir_lowering=False, num_devices=1)
    arrays, io = {}, {}
    given = {name: _np.ascontiguousarray(inputs[name]) for name in _INS}
    given.update(tables())
    for name, a in given.items():
        arrays[f"in_{name}"] = a
        io[name] = nc.dram_tensor(f"in_{name}", a.shape, _mybir.dt.from_np(a.dtype), kind="ExternalInput").ap()
    for name, shape in _OUTS:
        io[name] = nc.dram_tensor(f"out_{name}", shape, F32, kind="ExternalOutput").ap()
    build(nc, io)
    r = _run(nc, [arrays], core_ids=[0])
    return tuple(r.results[0][f"out_{name}"] for name, _ in _OUTS)
```
